# Optimizing a Trainium2 kernel written in Bass

```python
import math
import jax, jax.numpy as jnp
from jax import lax
import numpy as np

D_MODEL = 1024
BATCH = 1
SEQ = 256
DEPTH = 2
DEC_BATCH = 1
DEC_SEQ = 64
PAST_LEN = 256

CHUNK = 64
Q_BLOCK = 128
PLE_DIM = 256
EPS = 1e-6
A_HEADS = 8
A_DH = 64
A_DV = 2 * A_DH
A_QK = A_HEADS * 2 * A_DH
A_WIDTH = A_HEADS * A_DV
ROPE_DIM = A_DH // 4
ROPE_THETA = 500000.0
G_HEADS = 4
G_DK = D_MODEL // 2 // G_HEADS
G_DV = D_MODEL // G_HEADS
G_KW = G_HEADS * G_DK
G_VW = G_HEADS * G_DV
G_RANK = 16
G_NORMALIZER = 16.0
SUB = 16
D_FF = ((8 * D_MODEL // 3 + 255) // 256) * 256
IN_SPLITS = (A_QK, A_QK, A_WIDTH, G_KW, G_KW, G_VW, G_VW, G_RANK, D_MODEL, D_MODEL)
IN_WIDTH = A_QK + A_QK + A_WIDTH + G_KW + G_KW + G_VW + G_VW + G_RANK + D_MODEL + D_MODEL

kernel_name = 'chunk_stream_diffattn_gla_hybrid'

def rmsnorm(x, w):
    xf = x.astype(jnp.float32)
    y = xf * lax.rsqrt(jnp.mean(xf * xf, axis=-1, keepdims=True) + EPS)
    return (y * w.astype(jnp.float32)).astype(x.dtype)

def rope_partial(x, pos):
    half = ROPE_DIM // 2
    inv = ROPE_THETA ** (-jnp.arange(0, ROPE_DIM, 2, dtype=jnp.float32) / ROPE_DIM)
    ang = pos.astype(jnp.float32)[:, None] * inv[None, :]
    cos = jnp.cos(ang)[None, :, None, None, :]
    sin = jnp.sin(ang)[None, :, None, None, :]
    xr = x[..., :ROPE_DIM].astype(jnp.float32)
    x1, x2 = xr[..., :half], xr[..., half:]
    rot = jnp.concatenate([x1 * cos - x2 * sin, x2 * cos + x1 * sin], axis=-1)
    return jnp.concatenate([rot.astype(x.dtype), x[..., ROPE_DIM:]], axis=-1)

def diff_attend(q, k, v, lam, mask):
    s = jnp.einsum('bqhmd,bkhmd->bhmqk', q.astype(jnp.float32), k.astype(jnp.float32)) * (A_DH ** -0.5)
    if mask is not None:
        s = jnp.where(mask, s, -jnp.inf)
    p = jax.nn.softmax(s, axis=-1)
    a = p[:, :, 0] - lam * p[:, :, 1]
    return jnp.einsum('bhqk,bkhe->bqhe', a, v.astype(jnp.float32)).astype(v.dtype)

def diff_attend_prompt(q, k, v, lam):
    B, T = q.shape[0], q.shape[1]
    nqb = T // Q_BLOCK
    k_chunk = jnp.arange(T) // CHUNK
    qb = jnp.moveaxis(q.reshape(B, nqb, Q_BLOCK, A_HEADS, 2, A_DH), 1, 0)

    def one(args):
        q_blk, i = args
        q_chunk = (i * Q_BLOCK + jnp.arange(Q_BLOCK)) // CHUNK
        mask = k_chunk[None, :] <= q_chunk[:, None]
        return diff_attend(q_blk, k, v, lam, mask)

    o = lax.map(one, (qb, jnp.arange(nqb)))
    return jnp.moveaxis(o, 0, 1).reshape(B, T, A_HEADS, A_DV)

def gla_chunk(S, q, k, v, g):
    B, H, C, DK = q.shape
    DV = v.shape[-1]
    n = C // SUB
    b = jnp.cumsum(g, axis=2)
    o_state = jnp.einsum('bhcd,bhde->bhce', q * jnp.exp(b), S)
    bs = b.reshape(B, H, n, SUB, DK)
    qs = q.reshape(B, H, n, SUB, DK)
    ks = k.reshape(B, H, n, SUB, DK)
    vs = v.reshape(B, H, n, SUB, DV)
    r = jnp.concatenate([jnp.zeros((B, H, 1, DK), b.dtype), bs[:, :, :-1, -1]], axis=2)
    qf = qs * jnp.exp(bs - r[:, :, :, None, :])
    before = jnp.arange(C)[None, :] < (jnp.arange(n) * SUB)[:, None]
    ek = jnp.where(before[None, None, :, :, None], r[:, :, :, None, :] - b[:, :, None, :, :], -jnp.inf)
    kf = k[:, :, None] * jnp.exp(ek)
    a_inter = jnp.einsum('bhnid,bhncd->bhnic', qf, kf)
    o_inter = jnp.einsum('bhnic,bhce->bhnie', a_inter, v)
    tri = jnp.arange(SUB)[:, None] >= jnp.arange(SUB)[None, :]
    ed = jnp.where(tri[..., None], bs[:, :, :, :, None, :] - bs[:, :, :, None, :, :], -jnp.inf)
    a_intra = jnp.einsum('bhnid,bhnijd,bhnjd->bhnij', qs, jnp.exp(ed), ks)
    o_intra = jnp.einsum('bhnij,bhnje->bhnie', a_intra, vs)
    o = o_state + (o_inter + o_intra).reshape(B, H, C, DV)
    b_last = b[:, :, -1]
    S_new = jnp.exp(b_last)[..., None] * S + jnp.einsum('bhcd,bhce->bhde', k * jnp.exp(b_last[:, :, None] - b), v)
    return S_new, o

def gla_prompt(q, k, v, g):
    B, T = q.shape[0], q.shape[1]
    nc = T // CHUNK

    def to_chunks(a):
        a = a.astype(jnp.float32).transpose(0, 2, 1, 3)
        return jnp.moveaxis(a.reshape(B, G_HEADS, nc, CHUNK, a.shape[-1]), 2, 0)

    S0 = jnp.zeros((B, G_HEADS, G_DK, G_DV), jnp.float32)
    S, o = lax.scan(lambda S_c, xs: gla_chunk(S_c, xs[0], xs[1], xs[2], xs[3]), S0,
                    (to_chunks(q), to_chunks(k), to_chunks(v), to_chunks(g)))
    o = jnp.moveaxis(o, 0, 2).reshape(B, G_HEADS, T, G_DV).transpose(0, 2, 1, 3)
    return o, S

def gla_sample(q, k, v, g, S0):
    T = q.shape[1]
    pad = CHUNK - T

    def prep(a):
        a = jnp.pad(a.astype(jnp.float32), ((0, 0), (0, pad), (0, 0), (0, 0)))
        return a.transpose(0, 2, 1, 3)

    S, o = gla_chunk(S0.astype(jnp.float32), prep(q), prep(k), prep(v), prep(g))
    return o[:, :, :T].transpose(0, 2, 1, 3), S

def layer(x, pe, pos, l, attend, recur, lw):
    (w_in, norm_mix, lq1, lk1, lq2, lk2, a_subln, w_pa, w_ga2, b_ga, g_norm, w_pb, w_o,
     norm_ffn, w_f1, w_f3, w_f2, norm_ple, w_ple, w_ple_gate) = lw
    B, T = x.shape[0], x.shape[1]
    h = rmsnorm(x, norm_mix)
    z = h @ w_in
    idx = []
    acc = 0
    for s in IN_SPLITS[:-1]:
        acc += s
        idx.append(acc)
    qa, ka, va, qg, kg, vg, rg, ag, ga, gb = jnp.split(z, idx, axis=-1)
    qa = rope_partial(qa.reshape(B, T, A_HEADS, 2, A_DH), pos)
    ka = rope_partial(ka.reshape(B, T, A_HEADS, 2, A_DH), pos)
    va = va.reshape(B, T, A_HEADS, A_DV)
    lam_init = 0.8 - 0.6 * math.exp(-0.3 * l)
    f32 = jnp.float32
    lam = (jnp.exp(jnp.sum(lq1.astype(f32) * lk1.astype(f32)))
           - jnp.exp(jnp.sum(lq2.astype(f32) * lk2.astype(f32))) + lam_init)
    oa = attend(qa, ka, va, lam)
    oa = rmsnorm(oa, a_subln) * (1.0 - lam_init)
    ua = oa.reshape(B, T, A_WIDTH) @ w_pa
    g = jax.nn.log_sigmoid((ag @ w_ga2 + b_ga).astype(f32)) / G_NORMALIZER
    og, S = recur(qg.reshape(B, T, G_HEADS, G_DK) * (G_DK ** -0.5),
                  kg.reshape(B, T, G_HEADS, G_DK),
                  vg.reshape(B, T, G_HEADS, G_DV),
                  g.reshape(B, T, G_HEADS, G_DK))
    og = rmsnorm(og, g_norm).reshape(B, T, G_VW) * jax.nn.silu(rg)
    ub = og.astype(x.dtype) @ w_pb
    mixed = jax.nn.sigmoid(ga) * ua + jax.nn.sigmoid(gb) * ub
    x = x + (mixed @ w_o).astype(x.dtype)
    h = rmsnorm(x, norm_ffn)
    x = x + ((jax.nn.silu(h @ w_f1) * (h @ w_f3)) @ w_f2).astype(x.dtype)
    h = rmsnorm(x, norm_ple)
    x = x + (jax.nn.sigmoid(h @ w_ple_gate) * (pe @ w_ple)).astype(x.dtype)
    return x, ka.reshape(B, T, A_HEADS, A_DV), va, S

def setup_inputs(seed: int = 0) -> dict:
    key = jax.random.key(seed)
    ks = jax.random.split(key, 32)
    f32 = jnp.float32

    def nrm(k, shape, scale):
        return jax.random.normal(k, shape, f32) * scale

    def gain(k, shape):
        return 1.0 + 0.01 * jax.random.normal(k, shape, f32)

    return {
        'x_prompt': nrm(ks[0], (BATCH, SEQ, D_MODEL), 1.0),
        'x_sample': nrm(ks[1], (DEC_BATCH, DEC_SEQ, D_MODEL), 1.0),
        'p_prompt': nrm(ks[2], (DEPTH, BATCH, SEQ, PLE_DIM), 1.0),
        'p_sample': nrm(ks[3], (DEPTH, DEC_BATCH, DEC_SEQ, PLE_DIM), 1.0),
        'cache_k': nrm(ks[4], (DEPTH, DEC_BATCH, PAST_LEN, A_HEADS, A_DV), 1.0),
        'cache_v': nrm(ks[5], (DEPTH, DEC_BATCH, PAST_LEN, A_HEADS, A_DV), 1.0),
        'state_gla': nrm(ks[6], (DEPTH, DEC_BATCH, G_HEADS, G_DK, G_DV), 0.5),
        'w_in': nrm(ks[7], (DEPTH, D_MODEL, IN_WIDTH), D_MODEL ** -0.5),
        'norm_mix': gain(ks[8], (DEPTH, D_MODEL)),
        'lambda_q1': nrm(ks[9], (DEPTH, A_DH), 0.1),
        'lambda_k1': nrm(ks[10], (DEPTH, A_DH), 0.1),
        'lambda_q2': nrm(ks[11], (DEPTH, A_DH), 0.1),
        'lambda_k2': nrm(ks[12], (DEPTH, A_DH), 0.1),
        'a_subln': gain(ks[13], (DEPTH, A_DV)),
        'w_pa': nrm(ks[14], (DEPTH, A_WIDTH, D_MODEL), A_WIDTH ** -0.5),
        'w_ga2': nrm(ks[15], (DEPTH, G_RANK, G_KW), G_RANK ** -0.5),
        'b_ga': nrm(ks[16], (DEPTH, G_KW), 0.1),
        'g_norm': gain(ks[17], (DEPTH, G_DV)),
        'w_pb': nrm(ks[18], (DEPTH, G_VW, D_MODEL), G_VW ** -0.5),
        'w_o': nrm(ks[19], (DEPTH, D_MODEL, D_MODEL), D_MODEL ** -0.5),
        'norm_ffn': gain(ks[20], (DEPTH, D_MODEL)),
        'w_f1': nrm(ks[21], (DEPTH, D_MODEL, D_FF), D_MODEL ** -0.5),
        'w_f3': nrm(ks[22], (DEPTH, D_MODEL, D_FF), D_MODEL ** -0.5),
        'w_f2': nrm(ks[23], (DEPTH, D_FF, D_MODEL), D_FF ** -0.5),
        'norm_ple': gain(ks[24], (DEPTH, D_MODEL)),
        'w_ple': nrm(ks[25], (DEPTH, PLE_DIM, D_MODEL), PLE_DIM ** -0.5),
        'w_ple_gate': nrm(ks[26], (DEPTH, D_MODEL, D_MODEL), D_MODEL ** -0.5),
        'final_norm': gain(ks[27], (D_MODEL,)),
    }

def reference(x_prompt, x_sample, p_prompt, p_sample, cache_k, cache_v, state_gla,
              w_in, norm_mix, lambda_q1, lambda_k1, lambda_q2, lambda_k2, a_subln, w_pa,
              w_ga2, b_ga, g_norm, w_pb, w_o, norm_ffn, w_f1, w_f3, w_f2, norm_ple,
              w_ple, w_ple_gate, final_norm):
    T_p = x_prompt.shape[1]
    DB, T_s = x_sample.shape[0], x_sample.shape[1]
    P = cache_k.shape[2]
    pos_p = jnp.arange(T_p)
    pos_s = P + jnp.arange(T_s)
    xp, xs = x_prompt, x_sample
    kp_l, vp_l, sp_l, ks_l, vs_l, ss_l = [], [], [], [], [], []
    for l in range(DEPTH):
        lw = (w_in[l], norm_mix[l], lambda_q1[l], lambda_k1[l], lambda_q2[l], lambda_k2[l],
              a_subln[l], w_pa[l], w_ga2[l], b_ga[l], g_norm[l], w_pb[l], w_o[l],
              norm_ffn[l], w_f1[l], w_f3[l], w_f2[l], norm_ple[l], w_ple[l], w_ple_gate[l])
        xp, kp, vp, sp = layer(xp, p_prompt[l], pos_p, l, diff_attend_prompt, gla_prompt, lw)
        kc = cache_k[l].reshape(DB, P, A_HEADS, 2, A_DH)
        vc = cache_v[l]

        def attend_s(q, k, v, lam, kc=kc, vc=vc):
            return diff_attend(q, jnp.concatenate([kc.astype(k.dtype), k], axis=1),
                               jnp.concatenate([vc.astype(v.dtype), v], axis=1), lam, None)

        def recur_s(q, k, v, g, s0=state_gla[l]):
            return gla_sample(q, k, v, g, s0)

        xs, kn, vn, sn = layer(xs, p_sample[l], pos_s, l, attend_s, recur_s, lw)
        kp_l.append(kp); vp_l.append(vp); sp_l.append(sp)
        ks_l.append(kn); vs_l.append(vn); ss_l.append(sn)
    y_prompt = rmsnorm(xp, final_norm)
    y_sample = rmsnorm(xs, final_norm)
    k_prompt = jnp.stack(kp_l)
    v_prompt = jnp.stack(vp_l)
    s_prompt = jnp.stack(sp_l)
    k_sample = jnp.stack(ks_l)
    v_sample = jnp.stack(vs_l)
    s_sample = jnp.stack(ss_l)
    return (y_prompt, y_sample, k_prompt, v_prompt, s_prompt, k_sample, v_sample, s_sample)


_drawn_inputs = setup_inputs


def setup_inputs(seed=0):
    import zlib

    import numpy as np

    out = dict(_drawn_inputs(seed))
    spreads = {}
    factors = {'norm_mix': 3.308,
     'lambda_q1': 4.813,
     'a_subln': 48.342,
     'g_norm': 23.311,
     'norm_ffn': 6.546,
     'norm_ple': 64.0,
     'final_norm': 38.997,
     'cache_k': 8.0,
     'cache_v': 8.0,
     'lambda_q2': 4.812}
    for name, (base, spread) in spreads.items():
        noise = np.random.default_rng([zlib.crc32(name.encode()), seed]).standard_normal(out[name].shape)
        drawn = base * np.exp(spread * noise) if base else spread * noise
        out[name] = __import__('jax').numpy.asarray(drawn.astype(out[name].dtype))
    for name, factor in factors.items():
        out[name] = (out[name] * factor).astype(out[name].dtype)
    return out
```

```python
from contextlib import ExitStack

import concourse.bass as bass
from concourse import mybir

F32 = mybir.dt.float32
F32R = mybir.dt.float32r
ALU = mybir.AluOpType
ACT = mybir.ActivationFunctionType
AX = mybir.AxisListType

P = 128
DEPTH = 2
D = 1024
KC = D // P
TP, TS = 256, 64
T = TP + TS
PAST = 256
HEADS, DH, DV = 8, 64, 128
GH, GDK, GDV, RANK = 4, 128, 256, 16
CH = 64
NCH = T // CH
FF = 2816
FC = FF // P
PLE = 256
EPS = 1e-6
LEVELS = [32, 16, 8, 4, 2, 1]
NL = len(LEVELS)
UW = 256

C_Q, C_K, C_V = 0, 1024, 2048
C_QG, C_KG, C_VG, C_RG = 3072, 3584, 4096, 5120
C_AG, C_GA, C_GB = 6144, 6160, 7184
IN_W = 8208

MIX_IT, MIX_N = 4, 16
MRG_IT, MRG_N = 4, 4
OUT_IT, OUT_N = 2, 4
FUP_IT, FUP_N = 11, 4
FDN_IT, FDN_N = 2, 12
PLE_IT, PLE_N = 2, 4
MRG_0 = MIX_IT * MIX_N
OUT_0 = MRG_0 + MRG_IT * MRG_N
FUP_0 = OUT_0 + OUT_IT * OUT_N
FDN_0 = FUP_0 + FUP_IT * FUP_N
PLE_0 = FDN_0 + FDN_IT * FDN_N
TILES = PLE_0 + PLE_IT * PLE_N
RES_MRG = MRG_0
RES_FUP = RES_MRG + MRG_IT * MRG_N
RESULTS = RES_FUP + FUP_IT * FUP_N
FDN_K = [8, 8, 6]
CREDIT_TILE = 4
CREDIT_RES = 2

K_ID, K_ONE, K_COS, K_SIN, K_RST = 0, 128, 256, 576, 896
K_MASK = 1216
K_ID2 = K_MASK + (NL + 1) * CH
K_MQ = K_ID2 + 64
K_EPS = K_MQ + 128
K_A5 = K_EPS + 1
K_B5 = K_A5 + 5
K_LI = K_B5 + 5
K_OM = K_LI + DEPTH
NCONST = K_OM + DEPTH

R_MIX, R_FFN, R_PLE, R_FIN, R_SUB, R_GN, R_BG = 0, 16, 32, 48, 56, 58, 62
NPAR = 70
U_MIX, U_FFN, U_PLE, U_SUB, U_GN, U_BG, U_C5 = 0, 8, 16, 24, 25, 27, 31
NCUR = 36

SWAP = [8 + i for i in range(8)] + list(range(8)) + list(range(16, 32))


def wait_plain(eng, known, sem, value):
    value = eng.to_reg(value)
    eng.wait_ge(known, 16)
    eng.wait_ge(sem, value)


class Steps:

    def __init__(self, eng, sem, base, total):
        self.eng, self.sem, self.base, self.total, self.n = eng, sem, base, total, 0

    def put(self, ins):
        self.n += 1
        ins.then_inc(self.sem, 1)

    def wait(self):
        self.eng.wait_ge(self.sem, self.base + self.n)

    def close(self):
        assert self.n == self.total, (self.n, self.total)


def encoder(nc, A, O):
    w_in = A["w_in"].rearrange("l (c p) n -> p (l c) n", p=P)
    w_pa = A["w_pa"].rearrange("l (c p) n -> p (l c) n", p=P)
    w_pb = A["w_pb"].rearrange("l (c p) n -> p (l c) n", p=P)
    w_o = A["w_o"].rearrange("l (c p) n -> p (l c) n", p=P)
    w_f1 = A["w_f1"].rearrange("l (c p) n -> p (l c) n", p=P)
    w_f3 = A["w_f3"].rearrange("l (c p) n -> p (l c) n", p=P)
    w_f2 = A["w_f2"].rearrange("l (c p) n -> p (l c) n", p=P)
    w_gate = A["w_ple_gate"].rearrange("l (c p) n -> p (l c) n", p=P)
    w_ple = A["w_ple"].rearrange("l (c p) n -> p (l c) n", p=P)
    w_ga2 = A["w_ga2"].rearrange("l r n -> r l n")
    cache_k = A["cache_k"].rearrange("l b (c p) h e -> p (l b c) (h e)", p=P)
    cache_v = A["cache_v"].rearrange("l b (c p) h e -> p (l b c) (h e)", p=P)
    state_in = A["state_gla"].rearrange("l b h d e -> d (l b h) e")
    pe_p = A["p_prompt"].rearrange("l b (c p) n -> p (l b c) n", p=P)
    pe_s = A["p_sample"].rearrange("l b t n -> t (l b) n")
    x_p = A["x_prompt"].rearrange("b (c p) d -> p (b c) d", p=P)
    x_s = A["x_sample"].rearrange("b t d -> t (b d)")
    y_p = O["y_prompt"].rearrange("b (c p) d -> p (b c) d", p=P)
    y_s = O["y_sample"].rearrange("b t d -> t (b d)")
    kv_p = [O[n].rearrange("l b (c p) h e -> p (l b c) (h e)", p=P) for n in ("k_prompt", "v_prompt")]
    kv_s = [O[n].rearrange("l b t h e -> t (l b) (h e)") for n in ("k_sample", "v_sample")]
    st_p = O["s_prompt"].rearrange("l b h d e -> d (l b h) e")
    st_s = O["s_sample"].rearrange("l b h d e -> d (l b h) e")

    ctx = ExitStack()

    def sb(name, shape, dt=F32, where=ctx):
        return where.enter_context(nc.sbuf_tensor(name, shape, dt))

    def sem(name):
        return ctx.enter_context(nc.semaphore(name))

    xT = sb("xT", [P, KC, T])
    x_hi = sb("x_hi", [P, KC, T], F32R)
    x_lo = sb("x_lo", [P, KC, T], F32R)
    w_raw = sb("w_raw", [P, 2, KC, UW])
    w_hi = sb("w_hi", [P, 4, KC, P], F32R)
    w_lo = sb("w_lo", [P, 4, KC, P], F32R)
    cst = sb("cst", [P, NCONST])
    parT = sb("parT", [P, NPAR])
    c5 = sb("c5", [P, DEPTH, 5])
    cur = sb("cur", [P, NCUR])
    ssq = sb("ssq", [P, T])
    sqt = sb("sqt", [P, T])
    rstd = sb("rstd", [P, T])
    agT = sb("agT", [RANK, T])
    w_ag = sb("w_ag", [P, KC, RANK])
    w_agg = sb("w_agg", [P, KC, RANK])
    ga2 = sb("ga2", [RANK, GH * GDK])

    with ExitStack() as where:
        k_raw = sb("k_raw", [P, 2, UW], where=where)
        v_past = sb("v_past", [P, 2, UW], where=where)
        s_past = sb("s_past", [P, GDV], where=where)
        E = sb("E", [P, NL + 2, T], where=where)
        ebl = sb("ebl", [P, NCH], where=where)
        qg = sb("qg", [P, T], where=where)
        kg = sb("kg", [P, T], where=where)
        kdT = sb("kdT", [P, 3, P], where=where)
        vgT = sb("vgT", [P, 2, T], where=where)
        vg_tok = sb("vg_tok", [P, 3, GDV], where=where)
        a_msk = sb("a_msk", [P, NL + 1, CH], where=where)
        a_sum = sb("a_sum", [P, 3, CH], where=where)
        z = sb("z", [P, 2, T], where=where)
        rot = sb("rot", [P, 2, T], where=where)
        kr = sb("kr", [P, 2, T], where=where)
        qr = sb("qr", [P, 2, T], where=where)
        vz = sb("vz", [P, 2, T], where=where)
        kcT = sb("kcT", [P, 2, PAST], where=where)
        mx = sb("mx", [P, 5], where=where)
        nb = sb("nb", [P, 5], where=where)
        sums = sb("sums", [P, 5], where=where)
        coef = sb("coef", [P, 5], where=where)
        p0 = sb("p0", [P, 2, P], where=where)
        p1 = sb("p1", [P, 2, 2 * P], where=where)
        p_s = sb("p_s", [P, PAST + TS], where=where)
        dmat = sb("dmat", [P, TS], where=where)
        attT = sb("attT", [P, 576], where=where)
        o_sq = sb("o_sq", [P, T], where=where)
        rs = sb("rs", [P, 3, T], where=where)
        b16 = sb("b16", [P, GH, T], where=where)
        k_tok = sb("k_tok", [P, 3, UW], where=where)
        v_tok = sb("v_tok", [P, 3, UW], where=where)
        S = sb("S", [P, 4, GDV], where=where)
        S_smp = sb("S_smp", [P, GDV], where=where)
        gab = sb("gab", [P, 2 * KC, T], where=where)
        oag = sb("oag", [P, 2 * KC, T], where=where)
    o_sb, zr, og_t, sig, og_q = vz, vgT, z, rot, qr
    zg = E[:, 0:GH, :]
    lg = E[:, GH:2 * GH, :]
    with ExitStack() as where:
        b_hi = sb("b_hi", [P, 2 * KC, T], F32R, where=where)
        b_lo = sb("b_lo", [P, 2 * KC, T], F32R, where=where)
        m1 = sb("m1", [P, 2, T], where=where)
        m2 = sb("m2", [P, 2, T], where=where)
    with ExitStack() as where:
        h_hi = sb("h_hi", [P, FC, T], F32R, where=where)
        h_lo = sb("h_lo", [P, FC, T], F32R, where=where)
        f1z = sb("f1z", [P, 2, T], where=where)
        f3z = sb("f3z", [P, 2, T], where=where)
        gz = sb("gz", [P, T], where=where)
        gs = sb("gs", [P, T], where=where)
        pe_tok = sb("pe_tok", [P, 3, PLE], where=where)
        wple = sb("wple", [P, 2, 2, UW], where=where)
        peT = sb("peT", [P, 2, T], where=where)
    with ExitStack() as where:
        x_tok = sb("x_tok", [P, 3, D], where=where)
        par = sb("par", [NPAR, P], where=where)
        lrow = sb("lrow", [1, 4, DEPTH * DH], where=where)
        lprod = sb("lprod", [1, 2, DEPTH * DH], where=where)
        lsum = sb("lsum", [1, 2, DEPTH], where=where)
        lexp = sb("lexp", [1, 2, DEPTH], where=where)
        lneg = sb("lneg", [1, DEPTH], where=where)
        nlam = sb("nlam", [P, DEPTH], where=where)

    big = [ctx.enter_context(nc.psum_tensor(f"big{i}", [P, 512], F32)) for i in range(2)]
    X = [ctx.enter_context(nc.psum_tensor(f"X{i}", [P, 512], F32)) for i in range(6)]

    raw_in = [sem("raw_in0"), sem("raw_in1")]
    consts_in = sem("consts_in")
    par_in = sem("par_in")
    x_in = sem("x_in")
    lam_in = sem("lam_in")
    ag_in = sem("ag_in")
    k_raw_in = sem("k_raw_in")
    v_past_in = sem("v_past_in")
    s_past_in = sem("s_past_in")
    pe_in = sem("pe_in")
    wple_in = [sem("wple_in0"), sem("wple_in1")]
    stores_left = sem("stores_left")
    k_stored = sem("k_stored")
    v_stored = sem("v_stored")
    s_stored = sem("s_stored")
    y_stored = sem("y_stored")
    hi_ready = sem("hi_ready")
    lo_ready = sem("lo_ready")
    tile_done = sem("tile_done")
    result_read = sem("result_read")
    x_ready = sem("x_ready")
    ssq_ready = sem("ssq_ready")
    norm_sum = sem("norm_sum")
    rstd_ready = sem("rstd_ready")
    xhi_ready = sem("xhi_ready")
    xlo_ready = sem("xlo_ready")
    cur_ready = sem("cur_ready")
    agg_ready = sem("agg_ready")
    ag_done = sem("ag_done")
    agT_ready = sem("agT_ready")
    g_done = sem("g_done")
    zg_ready = sem("zg_ready")
    lg_ready = sem("lg_ready")
    bcur_ready = sem("bcur_ready")
    args_ready = sem("args_ready")
    decay_ready = sem("decay_ready")
    gla_qk_ready = sem("gla_qk_ready")
    vg_trans = sem("vg_trans")
    vg_copied = sem("vg_copied")
    u_done = sem("u_done")
    state_ready = sem("state_ready")
    pairs_done = sem("pairs_done")
    a_ready = sem("a_ready")
    og_done = sem("og_done")
    og_even = sem("og_even")
    og_squared = sem("og_squared")
    og_sum = sem("og_sum")
    og_rstd = sem("og_rstd")
    sig_ready = sem("sig_ready")
    shuffled = sem("shuffled")
    sin_ready = sem("sin_ready")
    rope_ready = sem("rope_ready")
    k_trans = sem("k_trans")
    k_copied = sem("k_copied")
    v_trans = sem("v_trans")
    v_copied = sem("v_copied")
    scores_done = sem("scores_done")
    negmax_ready = sem("negmax_ready")
    probs_ready = sem("probs_ready")
    maps_ready = sem("maps_ready")
    att_trans = sem("att_trans")
    att_copied = sem("att_copied")
    pv_done = sem("pv_done")
    o_squared = sem("o_squared")
    o_sum = sem("o_sum")
    o_rstd = sem("o_rstd")
    branch_ready = sem("branch_ready")
    gates_ready = sem("gates_ready")
    bhi_ready = sem("bhi_ready")
    blo_ready = sem("blo_ready")
    mixed_ready = sem("mixed_ready")
    mixhi_ready = sem("mixhi_ready")
    mixlo_ready = sem("mixlo_ready")
    silu_ready = sem("silu_ready")
    h_ready = sem("h_ready")
    hhi_ready = sem("hhi_ready")
    hlo_ready = sem("hlo_ready")
    pe_trans = sem("pe_trans")
    peT_ready = sem("peT_ready")
    ple_done = sem("ple_done")
    ple_used = sem("ple_used")
    gz_ready = sem("gz_ready")
    gs_ready = sem("gs_ready")
    par_trans = sem("par_trans")
    par_ready = sem("par_ready")
    x_trans = sem("x_trans")
    lsum_ready = sem("lsum_ready")
    lexp_ready = sem("lexp_ready")
    lneg_ready = sem("lneg_ready")
    lam_bc = sem("lam_bc")
    y_ready = sem("y_ready")
    y_trans = sem("y_trans")
    y_copied = [sem("y_copied_dve"), sem("y_copied_act")]
    dve_pro, dve_lay, dve_mix = sem("dve_pro"), sem("dve_lay"), sem("dve_mix")
    act_rms, act_decay, act_mix = sem("act_rms"), sem("act_decay"), sem("act_mix")
    pool_sq, pool_acc = sem("pool_sq"), sem("pool_acc")

    ident = cst[:, K_ID:K_ID + P]
    ones = cst[:, K_ONE:K_ONE + P]
    cos2 = cst[:, None, K_COS:K_COS + T].broadcast_to([P, 2, T])
    sin2 = cst[:, None, K_SIN:K_SIN + T].broadcast_to([P, 2, T])
    amask = cst[:, K_MASK:K_MASK + (NL + 1) * CH].rearrange("p (a b) -> p a b", a=NL + 1)

    def bc(ap, shape):
        return ap.broadcast_to(shape)

    def rows(tile):
        return TS if tile == 2 else P

    def halves(ap, h):
        v = ap.rearrange("p (n a h) -> p n a h", a=2, h=h)
        return v[:, :, 0, :], v[:, :, 1, :]

    block = ctx.enter_context(nc.Block())

    @block.sync
    def _(sp):
        sp.dma_start(cst[:, :], A["consts"]).then_inc(consts_in, 16)
        sp.dma_start(x_tok[:, 0:2, :], x_p).then_inc(x_in, 16)
        sp.dma_start(x_tok[0:TS, 2, :], x_s[:, :]).then_inc(x_in, 16)

        def unit(tb, c, src, row0, nrow, col0):
            sp.wait_ge(lo_ready, tb + (2 * c + CREDIT_TILE - 2))
            for r in range(0, nrow, nrow // 2):
                sp.dma_start(w_raw[:, c % 2, r:r + nrow // 2, :],
                             src[:, bass.ds(row0 + r, nrow // 2), bass.ds(col0, UW)]).then_inc(raw_in[c % 2], 16)

        def qk_unit(tb, l, j):
            sp.wait_ge(lo_ready, tb + (CREDIT_TILE - 2))
            for half, col in enumerate((C_QG, C_KG)):
                sp.dma_start(w_raw[:, 0, :, half * P:(half + 1) * P],
                             w_in[:, bass.ds(l * KC, KC), bass.ds(j * P + col, P)]).then_inc(raw_in[0], 16)

        with sp.Fori(0, DEPTH) as l:
            sp.dma_start(w_ag[:, :, :], w_in[:, bass.ds(l * KC, KC), C_AG:C_AG + RANK]).then_inc(ag_in, 16)
            sp.dma_start(ga2[:, None, :], w_ga2[:, bass.ds(l, 1), :]).then_inc(ag_in, 16)
            with sp.Fori(0, MIX_IT) as j:
                tb = sp.snap(l * TILES + j * MIX_N)
                qk_unit(tb, l, j)
                unit(tb, 1, w_in, l * KC, KC, j * UW + C_K)
                sp.wait_ge(x_trans, KC)
                sp.dma_start(k_raw[:, :, :], cache_k[:, bass.ds(l * 2, 2), bass.ds(j * UW, UW)]).then_inc(k_raw_in, 16)
                unit(tb, 2, w_in, l * KC, KC, j * UW + C_Q)
                unit(tb, 3, w_in, l * KC, KC, j * UW + C_VG)
                unit(tb, 4, w_in, l * KC, KC, j * UW + C_V)
                sp.dma_start(v_past[:, :, :], cache_v[:, bass.ds(l * 2, 2), bass.ds(j * UW, UW)]).then_inc(v_past_in, 16)
                sp.dma_start(s_past[:, None, :], state_in[:, bass.ds(l * GH + j, 1), :]).then_inc(s_past_in, 16)
                unit(tb, 5, w_in, l * KC, KC, j * UW + C_RG)
                unit(tb, 6, w_in, l * KC, KC, j * UW + C_GA)
                unit(tb, 7, w_in, l * KC, KC, j * UW + C_GB)
            with sp.Fori(0, MRG_IT) as j:
                tb = sp.snap(l * TILES + j * MRG_N + MRG_0)
                unit(tb, 0, w_pb, l * KC, KC, j * UW)
                unit(tb, 1, w_pa, l * KC, KC, j * UW)
            with sp.Fori(0, OUT_IT) as j:
                tb = sp.snap(l * TILES + j * OUT_N + OUT_0)
                unit(tb, 0, w_o, l * KC, KC, j * (2 * UW))
                unit(tb, 1, w_o, l * KC, KC, j * (2 * UW) + UW)
            with sp.Fori(0, FUP_IT) as j:
                tb = sp.snap(l * TILES + j * FUP_N + FUP_0)
                unit(tb, 0, w_f1, l * KC, KC, j * UW)
                unit(tb, 1, w_f3, l * KC, KC, j * UW)
            sp.wait_ge(stores_left, l * MIX_IT + (MIX_IT + 1))
            sp.dma_start(pe_tok[:, 0:2, :], pe_p[:, bass.ds(l * 2, 2), :]).then_inc(pe_in, 16)
            sp.dma_start(pe_tok[0:TS, 2:3, :], pe_s[:, bass.ds(l, 1), :]).then_inc(pe_in, 16)
            with sp.Fori(0, FDN_IT) as j:
                tb = sp.snap(l * TILES + j * FDN_N + FDN_0)
                for pair in range(2):
                    for k, nk in enumerate(FDN_K):
                        unit(tb, 3 * pair + k, w_f2, l * FC + KC * k, nk, j * (2 * UW) + pair * UW)
            with sp.Fori(0, PLE_IT) as j:
                tb = sp.snap(l * TILES + j * PLE_N + PLE_0)
                for c in range(2):
                    unit(tb, c, w_gate, l * KC, KC, j * (2 * UW) + c * UW)
                    sp.wait_ge(tile_done, tb + (2 * c + CREDIT_TILE - 2))
                    sp.dma_start(wple[:, c, :, :], w_ple[:, bass.ds(l * 2, 2),
                                                         bass.ds(j * (2 * UW) + c * UW, UW)]).then_inc(wple_in[c], 16)
        sp.wait_ge(lo_ready, DEPTH * TILES + CREDIT_TILE - 2)
        for r in range(0, KC, KC // 2):
            sp.dma_start(w_raw[:, 0, r:r + KC // 2, :], w_in[:, r:r + KC // 2, 0:UW]).then_inc(raw_in[0], 16)
        for t in range(3):
            sp.wait_ge(y_copied[0], t + 1)
            sp.wait_ge(y_copied[1], t + 1)
            dst = y_p[:, t, :] if t < 2 else y_s[:, :]
            sp.dma_start(dst, x_tok[0:rows(t), t, :]).then_inc(y_stored, 16)
        sp.wait_ge(y_stored, 48)

    @block.gpsimd
    def _(pool):
        for n, (key, r0, cnt) in enumerate((("norm_mix", R_MIX, 16), ("norm_ffn", R_FFN, 16), ("norm_ple", R_PLE, 16),
                                            ("a_subln", R_SUB, 2), ("g_norm", R_GN, 4), ("b_ga", R_BG, 8))):
            pool.dma_start(par[r0:r0 + cnt, :], A[key].rearrange("l (c p) -> (l c) p", p=P)).then_inc(par_in, 16)
        pool.dma_start(par[R_FIN:R_FIN + 8, :], A["final_norm"].rearrange("(c p) -> c p", p=P)).then_inc(par_in, 16)
        for n, key in enumerate(("lambda_q1", "lambda_k1", "lambda_q2", "lambda_k2")):
            pool.dma_start(lrow[:, n, :], A[key].rearrange("(a l) d -> a (l d)", a=1)).then_inc(lam_in, 16)
        pool.sem_inc(stores_left, 1)

        def clear_ssq(sums_seen):
            if sums_seen is not None:
                wait_plain(pool, consts_in, norm_sum, sums_seen)
            nc.gpsimd.memset(ssq[:, :], 0.0).then_inc(pool_acc, 1)

        def square(n, chunk):
            pool.wait_ge(pool_acc, n[1])
            wait_plain(pool, consts_in, x_ready, n[0] + 1)
            nc.gpsimd.tensor_tensor(sqt[:, None, :], xT[:, chunk, :], xT[:, chunk, :], ALU.mult).then_inc(pool_sq, 1)
            pool.wait_ge(pool_sq, n[0] + 1)
            nc.gpsimd.tensor_tensor(ssq[:, :], ssq[:, :], sqt[:, :], ALU.add).then_inc(pool_acc if n[2] else ssq_ready, 1)

        clear_ssq(None)
        for c in range(KC):
            square((c, c + 1, c < KC - 1), slice(c, c + 1))

        def squares_of_loop(l, norm, iters, per):
            clear_ssq(l * 3 + norm)
            with pool.Fori(0, iters - 1) as j:
                for t in range(per):
                    n = pool.snap(l * 24 + j * per + (8 * norm + t))
                    a = pool.snap(l * 24 + j * per + (8 * norm + t + 1))
                    square((n, a, True), bass.ds(j * per + t, 1))
            for t in range(per):
                c = (iters - 1) * per + t
                n = pool.snap(l * 24 + (8 * norm + c))
                square((n, n + 1, c < KC - 1), slice(c, c + 1))

        with pool.Fori(0, DEPTH) as l:
            with pool.Fori(0, MIX_IT) as j:
                v = pool.snap(l * MIX_IT + j + 1)
                k_count, v_count = pool.snap(v * 7 - 1), pool.snap(v * 4)
                b = E[:, NL + 1, :]
                pool.wait_ge(bcur_ready, v)
                for lev, h in enumerate(LEVELS):
                    first, second = halves(b, h)
                    o1, o2 = halves(E[:, lev, :], h)
                    ref = bc(first[:, :, h - 1:h], [P, T // (2 * h), h])
                    nc.gpsimd.tensor_tensor(o1, ref, first, ALU.subtract).then_inc(args_ready, 1)
                    nc.gpsimd.tensor_tensor(o2, second, ref, ALU.subtract).then_inc(args_ready, 1)
                bch = b.rearrange("p (n c) -> p n c", c=CH)
                nc.gpsimd.tensor_tensor(E[:, NL, :].rearrange("p (n c) -> p n c", c=CH),
                                        bc(bch[:, :, CH - 1:CH], [P, NCH, CH]), bch, ALU.subtract).then_inc(args_ready, 1)
                for n in range(2):
                    pool.wait_ge(shuffled, 2 * v + (n - 1))
                    nc.gpsimd.tensor_tensor(rot[:, :, :], rot[:, :, :], sin2, ALU.mult).then_inc(sin_ready, 1)
                for tok, copied, count, stored, which in ((k_tok, k_copied, k_count, k_stored, 0), (v_tok, v_copied, v_count, v_stored, 1)):
                    wait_plain(pool, consts_in, copied, count)
                    pool.dma_start(kv_p[which][:, bass.ds(l * 2, 2), bass.ds(j * UW, UW)], tok[:, 0:2, :]).then_inc(stored, 16)
                    pool.dma_start(kv_s[which][:, bass.ds(l, 1), bass.ds(j * UW, UW)], tok[0:TS, 2:3, :]).then_inc(stored, 16)
                wait_plain(pool, consts_in, state_ready, 5 * v)
                pool.dma_start(st_p[:, bass.ds(l * GH + j, 1), :], S[:, 3:4, :]).then_inc(s_stored, 16)
                pool.dma_start(st_s[:, bass.ds(l * GH + j, 1), :], S_smp[:, None, :]).then_inc(s_stored, 16)
                for stored in (k_stored, v_stored, s_stored):
                    pool.wait_ge(stored, v * 32)
                pool.sem_inc(stores_left, 1)
            squares_of_loop(l, 1, OUT_IT, 4)
            squares_of_loop(l, 2, FDN_IT, 4)
            squares_of_loop(l, 3, PLE_IT, 4)
        for stored in (k_stored, v_stored, s_stored):
            pool.wait_ge(stored, 32 * MIX_IT * DEPTH)

    @block.scalar
    def _(act):
        def hi(tb, tb8, t, nk):
            act.wait_ge(raw_in[(t // 2) % 2], tb8 + 32 * (t // 4 + 1))
            act.wait_ge(tile_done, tb + (t + 1))
            nc.scalar.activation(w_hi[:, t % 4, 0:nk, :], w_raw[:, (t // 2) % 2, 0:nk, (t % 2) * P:(t % 2 + 1) * P],
                                 ACT.Copy).then_inc(hi_ready, 1)

        def base(l, j, per, first):
            return act.snap(l * TILES + j * per + first), act.snap(l * (8 * TILES) + j * (8 * per) + 8 * first)

        def rms(out, src, n, scale, done, steps, arrived, count):
            act.wait_ge(arrived, count)
            steps.put(nc.scalar.activation(out, src[:, 0:T], ACT.Ln, scale=scale, bias=cst[:, K_EPS:K_EPS + 1]))
            steps.wait()
            nc.scalar.activation(out, out, ACT.Exp, scale=-0.5).then_inc(done, 1)

        def norm_input(l, s, col):
            for m in range(KC):
                if m == 0:
                    act.wait_ge(x_ready, l * 24 + (8 * s + KC))
                    act.wait_ge(cur_ready, l + 1)
                nc.scalar.activation(x_hi[:, m, :], xT[:, m, :], ACT.Copy, scale=cur[:, col + m:col + m + 1]).then_inc(xhi_ready, 1)
            steps = Steps(act, act_rms, l * 3 + s, 1)
            rms(rstd[:, :], X[0], None, 1.0 / D, rstd_ready, steps, norm_sum, l * 3 + (s + 1))
            steps.close()

        act.wait_ge(consts_in, 16)
        act.wait_ge(lsum_ready, 1)
        nc.scalar.activation(lexp[:, :, :], lsum[:, :, :], ACT.Exp).then_inc(lexp_ready, 1)
        for t in range(2):
            act.wait_ge(raw_in[0], 32)
            nc.scalar.activation(w_hi[:, t, :, :], w_raw[:, 0, :, t * P:(t + 1) * P], ACT.Copy).then_inc(hi_ready, 1)

        with act.Fori(0, DEPTH) as l:
            norm_input(l, 0, U_MIX)
            act.wait_ge(zg_ready, l + 1)
            steps = Steps(act, act_decay, l * 2, 2)
            steps.put(nc.scalar.activation(lg, zg, ACT.Abs))
            steps.wait()
            steps.put(nc.scalar.activation(lg, lg, ACT.Exp, scale=-1.0))
            steps.wait()
            steps.close()
            nc.scalar.activation(lg, lg, ACT.Ln, bias=cst[:, K_ONE:K_ONE + 1]).then_inc(lg_ready, 1)

            with act.Fori(0, MIX_IT) as j:
                tb, tb8 = base(l, j, MIX_N, 0)
                v = act.snap(l * MIX_IT + j + 1)
                st = Steps(act, act_mix, v * 5 - 5, 5)

                def at(per, k):
                    return v * per + (k - per)

                def exps(h):
                    act.wait_ge(negmax_ready, at(2, h + 1))
                    if h:
                        act.wait_ge(att_trans, at(2, 1))
                    for n, (dst, src) in enumerate(((p0[:, 0, :], X[4][:, 2 * P:3 * P]), (p0[:, 1, :], X[5][:, 2 * P:3 * P]),
                                                    (p1[:, 0, :], X[4][:, 0:2 * P]), (p1[:, 1, :], X[5][:, 0:2 * P]),
                                                    (p_s[:, :], X[0][:, 0:PAST + TS]))):
                        nc.scalar.activation(dst, src, ACT.Exp, bias=nb[:, n:n + 1], scale=DH ** -0.5,
                                             accum_out=sums[:, n:n + 1]).then_inc(probs_ready, 1)

                def att_copy(h):
                    act.wait_ge(att_trans, at(2, h + 1))
                    if h:
                        act.wait_ge(pv_done, at(2, 1))
                    src = X[3] if h == 0 else X[4]
                    nc.scalar.copy(attT[:, P:P + 384], src[:, 0:384]).then_inc(att_copied, 1)
                    nc.scalar.copy(attT[0:TS, 512:576], src[0:TS, 384:448]).then_inc(att_copied, 1)
                    nc.scalar.copy(attT[:, 0:P], X[0][:, 0:P]).then_inc(att_copied, 1)

                def o_copy(h, src):
                    act.wait_ge(pv_done, at(2, h + 1))
                    nc.scalar.copy(o_sb[:, h, :], src[:, 0:T]).then_inc(o_squared, 1)
                    if h:
                        act.wait_ge(o_sum, at(2, 1))
                    nc.scalar.activation(o_sq[:, :], src[:, 0:T], ACT.Square).then_inc(o_squared, 1)

                def tok_copy(dst, src, h, done):
                    nc.scalar.copy(dst[:, 0:2, h * P:(h + 1) * P], src[:, 0:2 * P].rearrange("p (a b) -> p a b", a=2)).then_inc(done, 1)
                    nc.scalar.copy(dst[0:TS, 2, h * P:(h + 1) * P], src[0:TS, 2 * P:3 * P]).then_inc(done, 1)

                for t in range(MIX_N):
                    hi(tb, tb8, t + 2, KC)
                    if t == 2:
                        act.wait_ge(args_ready, v * (2 * NL + 1))
                        nc.scalar.activation(E[:, 0:NL + 1, :], E[:, 0:NL + 1, :], ACT.Exp).then_inc(decay_ready, 1)
                        nc.scalar.activation(E[:, NL + 1, :], E[:, NL + 1, :], ACT.Exp).then_inc(decay_ready, 1)
                    if t == 5:
                        act.wait_ge(k_trans, at(4, 1))
                        tok_copy(kdT, X[0], 0, k_copied)
                        act.wait_ge(stores_left, v)
                        for h in range(2):
                            act.wait_ge(k_trans, at(4, 2 + h))
                            tok_copy(k_tok, X[1 + h], h, k_copied)
                        act.wait_ge(k_trans, at(4, 4))
                        nc.scalar.copy(kcT[:, :, :], X[3][:, :].rearrange("p (a b) -> p a b", a=2)).then_inc(k_copied, 1)
                    if t == 7:
                        exps(0)
                    if t == 10:
                        for e in range(2):
                            act.wait_ge(vg_trans, at(2, e + 1))
                            tok_copy(vg_tok, X[1 + e], e, vg_copied)
                        att_copy(0)
                    if t == 11:
                        for h in range(2):
                            act.wait_ge(v_trans, at(2, h + 1))
                            tok_copy(v_tok, X[1 + h], h, v_copied)
                        exps(1)
                    if t == 12:
                        act.wait_ge(result_read, l * RESULTS + j * MIX_N + (12 + CREDIT_RES))
                        st.put(nc.scalar.activation(sig[:, :, :], zr[:, :, :], ACT.Exp, scale=-1.0))
                        st.wait()
                        st.put(nc.scalar.activation(sig[:, :, :], sig[:, :, :], ACT.Ln, bias=cst[:, K_ONE:K_ONE + 1]))
                        st.wait()
                        nc.scalar.activation(sig[:, :, :], sig[:, :, :], ACT.Exp, scale=-1.0).then_inc(sig_ready, 1)
                    if t == 13:
                        o_copy(0, X[1])
                    if t == 14:
                        att_copy(1)
                    if t == 15:
                        for e in range(2):
                            act.wait_ge(og_done, at(2, e + 1))
                            nc.scalar.activation(og_q[:, e, :], X[2 + e][:, 0:T], ACT.Square).then_inc(og_squared, 1)
                        rms(rs[:, 0, :], X[1], None, 1.0 / DV, o_rstd, st, o_sum, at(2, 1))
                o_copy(1, X[0])
                rms(rs[:, 2, :], X[1], None, 1.0 / GDV, og_rstd, st, og_sum, v)
                rms(rs[:, 1, :], X[5], None, 1.0 / DV, o_rstd, st, o_sum, at(2, 2))
                st.close()

            for n, c in enumerate(list(range(KC, 2 * KC)) + list(range(KC))):
                if n == 0:
                    act.wait_ge(branch_ready, l * (3 * MIX_IT) + 3 * MIX_IT)
                nc.scalar.copy(b_hi[:, c, :], oag[:, c, :]).then_inc(bhi_ready, 1)
            act.wait_ge(result_read, l * RESULTS + (RES_MRG + CREDIT_RES))
            for c in (KC, 0):
                nc.scalar.activation(gab[:, c:c + KC, :], gab[:, c:c + KC, :], ACT.Sigmoid).then_inc(gates_ready, 1)
            with act.Fori(0, MRG_IT) as j:
                tb, tb8 = base(l, j, MRG_N, MRG_0)
                for t in range(MRG_N):
                    hi(tb, tb8, t + 2, KC)
                wait_plain(act, consts_in, mixed_ready, l * MRG_IT + j + 1)
                nc.scalar.copy(x_hi[:, bass.ds(j * 2, 2), :], m2[:, :, :]).then_inc(mixhi_ready, 1)
            with act.Fori(0, OUT_IT) as j:
                tb, tb8 = base(l, j, OUT_N, OUT_0)
                for t in range(OUT_N):
                    hi(tb, tb8, t + 2, KC)

            norm_input(l, 1, U_FFN)
            with act.Fori(0, FUP_IT) as j:
                tb, tb8 = base(l, j, FUP_N, FUP_0)
                for t in range(FUP_N):
                    hi(tb, tb8, t + 2, KC)
                    if t == 2:
                        act.wait_ge(result_read, l * RESULTS + j * FUP_N + (RES_FUP + 2 + CREDIT_RES))
                        nc.scalar.activation(f1z[:, :, :], f1z[:, :, :], ACT.Silu).then_inc(silu_ready, 1)
                wait_plain(act, consts_in, h_ready, l * FUP_IT + j + 1)
                nc.scalar.copy(h_hi[:, bass.ds(j * 2, 2), :], f3z[:, :, :]).then_inc(hhi_ready, 1)
            for c in range(2):
                act.wait_ge(pe_trans, l * 2 + (c + 1))
                nc.scalar.copy(peT[:, c, :], X[3 + c][:, 0:T]).then_inc(peT_ready, 1)
            with act.Fori(0, FDN_IT) as j:
                tb, tb8 = base(l, j, FDN_N, FDN_0)
                for t in range(FDN_N):
                    hi(tb, tb8, t + 2, FDN_K[(t + 2) // 2 % 3])

            norm_input(l, 2, U_PLE)
            with act.Fori(0, PLE_IT) as j:
                tb, tb8 = base(l, j, PLE_N, PLE_0)
                for t in range(PLE_N):
                    hi(tb, tb8, t + 2, KC)
                    act.wait_ge(gz_ready, l * KC + j * PLE_N + (t + 1 + CREDIT_RES))
                    nc.scalar.activation(gs[:, :], gz[:, :], ACT.Sigmoid).then_inc(gs_ready, 1)

        steps = Steps(act, act_rms, 3 * DEPTH, 1)
        rms(rstd[:, :], X[0], None, 1.0 / D, rstd_ready, steps, norm_sum, 3 * DEPTH + 1)
        for t in range(3):
            act.wait_ge(y_trans, 2 * t + 2)
            nc.scalar.copy(x_tok[0:rows(t), t, 512:1024], X[(2 * t + 1) % 6][0:rows(t), :]).then_inc(y_copied[1], 1)

    @block.vector
    def _(dve):
        dve.sem_inc(lo_ready, CREDIT_TILE)
        dve.sem_inc(result_read, CREDIT_RES)
        dve.sem_inc(ple_used, 2)
        dve.sem_inc(gz_ready, CREDIT_RES)
        tt = nc.vector.tensor_tensor
        stt = nc.vector.scalar_tensor_tensor

        def lo(tb, t, nk):
            dve.wait_ge(hi_ready, tb + (t + 1))
            tt(w_lo[:, t % 4, 0:nk, :], w_raw[:, (t // 2) % 2, 0:nk, (t % 2) * P:(t % 2 + 1) * P],
               w_hi[:, t % 4, 0:nk, :].bitcast(F32), ALU.subtract).then_inc(lo_ready, 1)

        def lo_input(l, s, col):
            for m in range(KC):
                dve.wait_ge(xhi_ready, l * 24 + (8 * s + m + 1))
                stt(x_lo[:, m, :], xT[:, m, :], cur[:, col + m:col + m + 1], x_hi[:, m, :].bitcast(F32),
                    ALU.mult, ALU.subtract).then_inc(xlo_ready, 1)

        st = Steps(dve, dve_pro, 0, 8)
        dve.wait_ge(consts_in, 16)
        dve.wait_ge(par_trans, 1)
        st.put(nc.vector.tensor_copy(parT[:, :], X[4][:, 0:NPAR]))
        st.wait()
        st.put(tt(parT[:, R_SUB:R_SUB + DEPTH], parT[:, R_SUB:R_SUB + DEPTH], cst[:, K_OM:K_OM + DEPTH], ALU.mult))
        dve.wait_ge(lam_in, 64)
        for n in range(2):
            st.put(tt(lprod[:, n, :], lrow[:, 2 * n, :], lrow[:, 2 * n + 1, :], ALU.mult))
        st.wait()
        nc.vector.tensor_reduce(lsum[:, :, :], lprod[:, :, :].rearrange("p a (l d) -> p a l d", l=DEPTH), AX.X, ALU.add).then_inc(lsum_ready, 1)
        dve.wait_ge(lexp_ready, 1)
        st.put(tt(lneg[:, :], lexp[:, 1, :], lexp[:, 0, :], ALU.subtract))
        st.wait()
        tt(lneg[:, :], lneg[:, :], cst[0:1, K_LI:K_LI + DEPTH], ALU.subtract).then_inc(lneg_ready, 1)
        dve.wait_ge(lam_bc, 1)
        st.put(nc.vector.tensor_copy(nlam[:, :], X[5][:, 0:DEPTH]))
        st.wait()
        for l in range(DEPTH):
            st.put(stt(c5[:, l, :], cst[:, K_B5:K_B5 + 5], nlam[:, l:l + 1], cst[:, K_A5:K_A5 + 5], ALU.mult, ALU.add))
        st.close()
        for m in range(KC):
            dve.wait_ge(x_trans, m + 1)
            nc.vector.tensor_copy(xT[:, m, :], X[m % 4][:, 0:T]).then_inc(x_ready, 1)
        for t in range(2):
            lo(0, t, KC)
        st.wait()

        with dve.Fori(0, DEPTH) as l:
            for dst, src, n in ((U_MIX, R_MIX, 8), (U_FFN, R_FFN, 8), (U_PLE, R_PLE, 8), (U_SUB, R_SUB, 1),
                                (U_GN, R_GN, 2), (U_BG, R_BG, 4)):
                nc.vector.tensor_copy(cur[:, dst:dst + n], parT[:, bass.ds(l * n + src, n)])
            nc.vector.tensor_copy(cur[:, None, U_C5:U_C5 + 5], c5[:, bass.ds(l, 1), :]).then_inc(cur_ready, 1)
            dve.wait_ge(cur_ready, l + 1)
            dve.wait_ge(ag_in, l * 32 + 32)
            tt(w_agg[:, :, :], w_ag[:, :, :], bc(cur[:, U_MIX:U_MIX + KC, None], [P, KC, RANK]), ALU.mult).then_inc(agg_ready, 1)
            lo_input(l, 0, U_MIX)
            dve.wait_ge(ag_done, l + 1)
            dve.wait_ge(rstd_ready, l * 3 + 1)
            tt(agT[:, :], X[1][0:RANK, 0:T], rstd[0:RANK, :], ALU.mult).then_inc(agT_ready, 1)
            dve.wait_ge(g_done, l + 1)
            for h in range(GH):
                ins = nc.vector.tensor_scalar(zg[:, h, :], X[2 + h][:, 0:T], cur[:, U_BG + h:U_BG + h + 1], None, ALU.add)
            ins.then_inc(zg_ready, 1)
            dve.wait_ge(lg_ready, l + 1)
            st = Steps(dve, dve_lay, l * (1 + GH), 1 + GH)
            st.put(stt(zg, zg, 0.0, lg, ALU.min, ALU.subtract))
            st.wait()
            for h in range(GH):
                st.put(nc.vector.tensor_tensor_scan(b16[:, h, :], cst[:, K_RST:K_RST + T], zg[:, h, :], 0.0, ALU.mult, ALU.add))
            wait_plain(dve, consts_in, dve_lay, l * (1 + GH) + (1 + GH))
            st.close()

            with dve.Fori(0, MIX_IT) as j:
                tb = dve.snap(l * TILES + j * MIX_N)
                rb = dve.snap(l * RESULTS + j * MIX_N)
                v = dve.snap(l * MIX_IT + j + 1)
                st = Steps(dve, dve_mix, v * 17 - 17, 17)

                def at(per, k):
                    return v * per + (k - per)

                def result(t):
                    dve.wait_ge(tile_done, tb + (t + 1 + CREDIT_TILE))

                def out_tile(dst, t):
                    result(t)
                    tt(dst, big[t % 2][:, 0:T], rstd[:, :], ALU.mult).then_inc(result_read, 1)

                def written(t):
                    wait_plain(dve, consts_in, result_read, rb + (t + 1 + CREDIT_RES))

                def rope(dst, n):
                    nc.vector.stream_shuffle(rot[:, :, :], z[:, :, :], SWAP).then_inc(shuffled, 1)
                    st.put(tt(dst[:, :, :], z[:, :, :], cos2, ALU.mult))
                    st.wait()
                    dve.wait_ge(sin_ready, at(2, n + 1))
                    tt(dst[:, :, :], dst[:, :, :], rot[:, :, :], ALU.add).then_inc(rope_ready, 1)

                def negmax(h):
                    dve.wait_ge(scores_done, at(2, h + 1))
                    for m in range(2):
                        nc.vector.tensor_reduce(mx[:, m:m + 1], X[4 + m][:, 2 * P:3 * P], AX.X, ALU.max)
                        nc.vector.tensor_reduce(mx[:, 2 + m:3 + m], X[4 + m][:, 0:2 * P], AX.X, ALU.max)
                    st.put(nc.vector.tensor_reduce(mx[:, 4:5], X[0][:, 0:PAST + TS], AX.X, ALU.max))
                    st.wait()
                    nc.vector.tensor_scalar(nb[:, :], mx[:, :], -DH ** -0.5, None, ALU.mult).then_inc(negmax_ready, 1)

                def difference(h):
                    dve.wait_ge(probs_ready, at(10, 5 * h + 5))
                    st.put(nc.vector.reciprocal(coef[:, :], sums[:, :]))
                    st.wait()
                    st.put(tt(coef[:, :], coef[:, :], cur[:, U_C5:U_C5 + 5], ALU.mult))
                    st.wait()
                    nc.vector.tensor_scalar(p0[:, 0, :], p0[:, 0, :], coef[:, 0:1], None, ALU.mult)
                    st.put(nc.vector.tensor_scalar(p1[:, 0, :], p1[:, 0, :], coef[:, 2:3], None, ALU.mult))
                    st.wait()
                    stt(p0[:, 0, :], p0[:, 1, :], coef[:, 1:2], p0[:, 0, :], ALU.mult, ALU.add)
                    stt(p1[:, 0, :], p1[:, 1, :], coef[:, 3:4], p1[:, 0, :], ALU.mult, ALU.add)
                    nc.vector.tensor_scalar(dmat[:, :], cst[:, K_ID2:K_ID2 + TS], coef[:, 4:5], None, ALU.mult).then_inc(maps_ready, 1)

                def state(c, dst, old, src):
                    stt(dst, old, ebl[:, c:c + 1], src, ALU.mult, ALU.add).then_inc(state_ready, 1)
                    dve.wait_ge(state_ready, at(5, {0: 1, 1: 2, 2: 3, 3: 4, 4: 5}[c]))

                for t in range(MIX_N):
                    lo(tb, t + 2, KC)
                    if t == 0:
                        nc.vector.tensor_scalar(E[:, NL + 1:NL + 2, :], b16[:, bass.ds(j, 1), :], 1.0 / 16.0, None, ALU.mult).then_inc(bcur_ready, 1)
                        result(0)
                        stt(qg[:, :], big[0][:, 0:T], GDK ** -0.5, rstd[:, :], ALU.mult, ALU.mult).then_inc(result_read, 1)
                    if t == 1:
                        out_tile(kg[:, :], t)
                    if t == 2:
                        out_tile(z[:, 0, :], t)
                    if t == 3:
                        dve.wait_ge(decay_ready, 2 * v)
                        written(1)
                        st.put(nc.vector.tensor_copy(ebl[:, :], E[:, NL + 1, CH - 1::CH]))
                        for lev, h in enumerate(LEVELS):
                            (e1, e2), (k1, _), (_, q2) = halves(E[:, lev, :], h), halves(kg[:, :], h), halves(qg[:, :], h)
                            tt(e1, e1, k1, ALU.mult)
                            tt(e2, e2, q2, ALU.mult)
                        tt(E[:, NL, :], E[:, NL, :], kg[:, :], ALU.mult)
                        st.wait()
                        tt(E[:, NL + 1, :], E[:, NL + 1, :], qg[:, :], ALU.mult).then_inc(gla_qk_ready, 1)
                        out_tile(z[:, 1, :], t)
                        written(3)
                        rope(kr, 0)
                    if t == 4:
                        out_tile(z[:, 0, :], t)
                    if t == 5:
                        out_tile(z[:, 1, :], t)
                        written(5)
                        rope(qr, 1)
                    if t in (6, 7):
                        if t == 7:
                            negmax(0)
                        out_tile(vgT[:, t - 6, :], t)
                    if t in (8, 9):
                        if t == 8:
                            for pair in range(3):
                                n = rows(pair)
                                dve.wait_ge(pairs_done, at(3, pair + 1))
                                if pair:
                                    dve.wait_ge(a_ready, at(3, pair))
                                st.put(tt(a_msk[0:n, :, :], X[1 + pair][0:n, 0:(NL + 1) * CH].rearrange("p (a b) -> p a b", a=NL + 1),
                                          amask[0:n, :, :], ALU.mult))
                                st.wait()
                                nc.vector.tensor_reduce(a_sum[0:n, pair, :], a_msk[0:n, :, :].rearrange("p a b -> p b a"), AX.X, ALU.add).then_inc(a_ready, 1)
                            difference(0)
                        out_tile(vz[:, t - 8, :], t)
                    if t in (10, 11):
                        if t == 10:
                            dve.wait_ge(vg_trans, 2 * v)
                        else:
                            negmax(1)
                        out_tile(zr[:, t - 10, :], t)
                    if t >= 12:
                        if t == 12:
                            dve.wait_ge(stores_left, v)
                            dve.wait_ge(u_done, at(3, 1))
                            nc.vector.tensor_copy(S[:, 0, :], X[3][:, 0:GDV]).then_inc(state_ready, 1)
                            dve.wait_ge(state_ready, at(5, 1))
                            difference(1)
                        if t == 13:
                            dve.wait_ge(u_done, at(3, 2))
                            state(1, S[:, 1, :], S[:, 0, :], X[2][:, 0:GDV])
                            state(2, S[:, 2, :], S[:, 1, :], X[3][:, GDV:2 * GDV])
                            state(3, S[:, 3, :], S[:, 2, :], X[2][:, GDV:2 * GDV])
                        if t == 14:
                            dve.wait_ge(u_done, at(3, 3))
                            dve.wait_ge(s_past_in, 16 * v)
                            state(4, S_smp[:, :], s_past[:, :], X[5][:, 0:GDV])
                        if t == 15:
                            dve.wait_ge(sig_ready, v)
                            st.put(tt(zr[:, :, :], zr[:, :, :], sig[:, :, :], ALU.mult))
                        c = (t - 12) if t < 14 else (KC + t - 14)
                        result(t)
                        tt(gab[:, bass.ds(j * 2 + c, 1), :], big[t % 2][:, None, 0:T], rstd[:, None, :], ALU.mult).then_inc(result_read, 1)
                def head_out(h):
                    dve.wait_ge(o_rstd, at(2, h + 1))
                    stt(oag[:, bass.ds(j * 2 + h, 1), :], o_sb[:, h:h + 1, :], cur[:, U_SUB:U_SUB + 1], rs[:, h:h + 1, :],
                        ALU.mult, ALU.mult).then_inc(branch_ready, 1)
                head_out(0)
                dve.wait_ge(og_rstd, v)
                for e in range(2):
                    st.put(stt(og_t[:, e, :], X[2 + e][:, 0:T], cur[:, U_GN + e:U_GN + e + 1], rs[:, 2, :], ALU.mult, ALU.mult))
                st.wait()
                tt(oag[:, bass.ds(j * 2 + KC, 2), :], og_t[:, :, :], zr[:, :, :], ALU.mult).then_inc(branch_ready, 1)
                head_out(1)
                st.close()

            for n, c in enumerate(list(range(KC, 2 * KC)) + list(range(KC))):
                dve.wait_ge(bhi_ready, l * (2 * KC) + (n + 1))
                tt(b_lo[:, c, :], oag[:, c, :], b_hi[:, c, :].bitcast(F32), ALU.subtract).then_inc(blo_ready, 1)
            with dve.Fori(0, MRG_IT) as j:
                tb = dve.snap(l * TILES + j * MRG_N + MRG_0)
                rb = dve.snap(l * RESULTS + j * MRG_N + RES_MRG)
                for t in range(MRG_N):
                    lo(tb, t + 2, KC)
                    dve.wait_ge(gates_ready, l * 2 + (t // 2 + 1))
                    dve.wait_ge(tile_done, tb + (t + 1 + CREDIT_TILE))
                    c = t % 2 + (KC if t < 2 else 0)
                    tt((m1 if t < 2 else m2)[:, t % 2:t % 2 + 1, :], big[t % 2][:, None, 0:T], gab[:, bass.ds(j * 2 + c, 1), :],
                       ALU.mult).then_inc(result_read, 1)
                dve.wait_ge(result_read, rb + (MRG_N + CREDIT_RES))
                tt(m2[:, :, :], m2[:, :, :], m1[:, :, :], ALU.add).then_inc(mixed_ready, 1)
                dve.wait_ge(mixed_ready, l * MRG_IT + j + 1)
                dve.wait_ge(mixhi_ready, l * MRG_IT + j + 1)
                tt(x_lo[:, bass.ds(j * 2, 2), :], m2[:, :, :], x_hi[:, bass.ds(j * 2, 2), :].bitcast(F32), ALU.subtract).then_inc(mixlo_ready, 1)
            with dve.Fori(0, OUT_IT) as j:
                tb = dve.snap(l * TILES + j * OUT_N + OUT_0)
                for t in range(OUT_N):
                    lo(tb, t + 2, KC)
                    dve.wait_ge(tile_done, tb + (t + 1 + CREDIT_TILE))
                    x = xT[:, bass.ds(j * 4 + t, 1), :]
                    tt(x, big[t % 2][:, None, 0:T], x, ALU.add).then_inc(x_ready, 1)

            lo_input(l, 1, U_FFN)
            wait_plain(dve, consts_in, rstd_ready, l * 3 + 2)
            with dve.Fori(0, FUP_IT) as j:
                tb = dve.snap(l * TILES + j * FUP_N + FUP_0)
                rb = dve.snap(l * RESULTS + j * FUP_N + RES_FUP)
                for t in range(FUP_N):
                    lo(tb, t + 2, KC)
                    dve.wait_ge(tile_done, tb + (t + 1 + CREDIT_TILE))
                    tt((f1z if t < 2 else f3z)[:, t % 2, :], big[t % 2][:, 0:T], rstd[:, :], ALU.mult).then_inc(result_read, 1)
                dve.wait_ge(result_read, rb + (FUP_N + CREDIT_RES))
                dve.wait_ge(silu_ready, l * FUP_IT + j + 1)
                tt(f3z[:, :, :], f3z[:, :, :], f1z[:, :, :], ALU.mult).then_inc(h_ready, 1)
                dve.wait_ge(h_ready, l * FUP_IT + j + 1)
                dve.wait_ge(hhi_ready, l * FUP_IT + j + 1)
                tt(h_lo[:, bass.ds(j * 2, 2), :], f3z[:, :, :], h_hi[:, bass.ds(j * 2, 2), :].bitcast(F32), ALU.subtract).then_inc(hlo_ready, 1)
            with dve.Fori(0, FDN_IT) as j:
                tb = dve.snap(l * TILES + j * FDN_N + FDN_0)
                for t in range(FDN_N):
                    lo(tb, t + 2, FDN_K[(t + 2) // 2 % 3])
                    if t // 2 % 3 == 2:
                        dve.wait_ge(tile_done, tb + (t + 1 + CREDIT_TILE))
                        x = xT[:, bass.ds(j * 4 + (t // 6 * 2 + t % 2), 1), :]
                        tt(x, big[t % 2][:, None, 0:T], x, ALU.add).then_inc(x_ready, 1)

            lo_input(l, 2, U_PLE)
            wait_plain(dve, consts_in, rstd_ready, l * 3 + 3)
            with dve.Fori(0, PLE_IT) as j:
                tb = dve.snap(l * TILES + j * PLE_N + PLE_0)
                n8 = dve.snap(l * KC + j * PLE_N)
                for t in range(PLE_N):
                    lo(tb, t + 2, KC)
                    dve.wait_ge(tile_done, tb + (t + 1 + CREDIT_TILE))
                    tt(gz[:, :], big[t % 2][:, 0:T], rstd[:, :], ALU.mult).then_inc(gz_ready, 1)
                    dve.wait_ge(gs_ready, n8 + (t + 1))
                    dve.wait_ge(ple_done, n8 + (t + 1))
                    tt(gs[:, :], gs[:, :], X[1 + t % 2][:, 0:T], ALU.mult).then_inc(ple_used, 1)
                    dve.wait_ge(ple_used, n8 + (t + 1 + 2))
                    x = xT[:, bass.ds(j * 4 + t, 1), :]
                    tt(x, x, gs[:, None, :], ALU.add).then_inc(x_ready, 1)

        dve.wait_ge(rstd_ready, 3 * DEPTH + 1)
        for m in range(KC):
            stt(xT[:, m, :], xT[:, m, :], parT[:, R_FIN + m:R_FIN + m + 1], rstd[:, :], ALU.mult, ALU.mult).then_inc(y_ready, 1)
        for t in range(3):
            dve.wait_ge(y_trans, 2 * t + 1)
            nc.vector.tensor_copy(x_tok[0:rows(t), t, 0:512], X[2 * t][0:rows(t), :]).then_inc(y_copied[0], 1)

    @block.tensor
    def _(pe):
        mm = nc.tensor.matmul
        pe.sem_inc(tile_done, CREDIT_TILE)

        def tile(tb, t, xh, xl, k0=0, nk=KC, start=True, stop=True, chunk_wait=None):
            pe.wait_ge(lo_ready, tb + (t + 1 + CREDIT_TILE))
            out = big[t % 2][:, 0:T]
            for k in range(nk):
                if chunk_wait is not None:
                    pe.wait_ge(xlo_ready, chunk_wait + (k + 1))
                wh, wl = w_hi[:, t % 4, k, :], w_lo[:, t % 4, k, :]
                mm(out, wh, xh[:, k0 + k, :], start=start and k == 0, stop=False)
                mm(out, wh, xl[:, k0 + k, :], start=False, stop=False)
                last = mm(out, wl, xh[:, k0 + k, :], start=False, stop=stop and k == nk - 1)
            last.then_inc(tile_done, 1)

        def transposes(out, srcs, n):
            for i in range(3):
                last = nc.tensor.transpose(out[0:rows(i), i * P:(i + 1) * P], srcs[:, i * P:i * P + rows(i)], ident)
            return last

        def norm_sums(count):
            pe.wait_ge(ssq_ready, count)
            mm(X[0][:, 0:T], ones, ssq[:, :], start=True, stop=True).then_inc(norm_sum, 1)

        pe.wait_ge(consts_in, 16)
        pe.wait_ge(par_in, 112)
        nc.tensor.transpose(X[4][:, 0:NPAR], par[:, :], ident[0:NPAR, 0:NPAR]).then_inc(par_trans, 1)
        pe.wait_ge(x_in, 32)
        for m in range(KC):
            if m >= 4:
                pe.wait_ge(x_ready, m - 3)
            for i in range(3):
                n = rows(i)
                last = nc.tensor.transpose(X[m % 4][:, i * P:i * P + n], x_tok[0:n, i, m * P:(m + 1) * P], ident[0:n, 0:n])
            last.then_inc(x_trans, 1)
            if m == 3:
                pe.wait_ge(lneg_ready, 1)
                mm(X[5][:, 0:DEPTH], ones[0:1, :], lneg[:, :], start=True, stop=True).then_inc(lam_bc, 1)

        with pe.Fori(0, DEPTH) as l:
            pe.wait_ge(x_ready, l * 24 + 8)
            pe.wait_ge(agg_ready, l + 1)
            for k in range(KC):
                last = mm(X[1][0:RANK, 0:T], w_agg[:, k, :], xT[:, k, :], start=k == 0, stop=k == KC - 1)
            last.then_inc(ag_done, 1)
            norm_sums(l * 3 + 1)
            pe.wait_ge(agT_ready, l + 1)
            for h in range(GH):
                last = mm(X[2 + h][:, 0:T], ga2[:, h * GDK:(h + 1) * GDK], agT[:, :], start=True, stop=True)
            last.then_inc(g_done, 1)

            with pe.Fori(0, MIX_IT) as j:
                tb = pe.snap(l * TILES + j * MIX_N)
                rb = pe.snap(l * RESULTS + j * MIX_N)
                v = pe.snap(l * MIX_IT + j + 1)
                xc = pe.snap(l * 24)

                def at(per, k):
                    return v * per + (k - per)

                def scores(h):
                    q, k, kc = qr[:, h, :], kr[:, h, :], kcT[:, h, :]
                    mq = cst[0:1, K_MQ:K_MQ + P]
                    for m in range(2):
                        r = slice(m * DH, (m + 1) * DH)
                        for at0, q0, nk in ((0, P, 2 * P), (2 * P, 0, P)):
                            last64 = X[4 + m][:, at0 + nk - CH:at0 + nk]
                            mm(X[4 + m][:, at0:at0 + nk - CH], q[r, q0:q0 + P], k[r, 0:nk - CH], start=True, stop=True)
                            mm(last64, q[r, q0:q0 + P], k[r, nk - CH:nk], start=True, stop=False)
                            mm(last64, mq, cst[0:1, K_ONE:K_ONE + CH], start=False, stop=True)
                    for m in range(2):
                        r = slice(m * DH, (m + 1) * DH)
                        mm(X[0][r, 0:PAST], q[r, TP:T], kc[r, :], start=True, stop=True)
                        last = mm(X[0][r, PAST:PAST + TS], q[r, TP:T], k[r, TP:T], start=True, stop=True)
                    last.then_inc(scores_done, 1)

                def att_transposes(h):
                    out = X[3] if h == 0 else X[4]
                    pe.wait_ge(maps_ready, at(2, h + 1))
                    for i in range(2):
                        nc.tensor.transpose(out[:, i * P:(i + 1) * P], p1[:, 0, i * P:(i + 1) * P], ident)
                    nc.tensor.transpose(X[0][:, 0:P], p0[:, 0, :], ident)
                    for i in range(3):
                        n = rows(i)
                        last = mm(out[0:n, 2 * P + i * TS:2 * P + (i + 1) * TS], p_s[:, i * P:i * P + n], dmat[:, :], start=True, stop=True)
                    last.then_inc(att_trans, 1)

                def values(h, out):
                    c = slice(h * P, (h + 1) * P)
                    pe.wait_ge(att_copied, at(6, 3 * h + 3))
                    mm(out[:, 0:P], v_tok[:, 0, c], attT[:, 0:P], start=True, stop=True)
                    mm(out[:, P:2 * P], v_tok[:, 0, c], attT[:, P:2 * P], start=True, stop=False)
                    mm(out[:, P:2 * P], v_tok[:, 1, c], attT[:, 2 * P:3 * P], start=False, stop=True)
                    mm(out[:, TP:T], v_past[:, 0, c], attT[:, 384:448], start=True, stop=False)
                    mm(out[:, TP:T], v_past[:, 1, c], attT[:, 448:512], start=False, stop=False)
                    mm(out[:, TP:T], v_tok[0:TS, 2, c], attT[0:TS, 512:576], start=False, stop=True).then_inc(pv_done, 1)

                def chunk_rows(c):
                    return slice((c % 2) * CH, (c % 2) * CH + CH)

                def own_sum(c, out):
                    return mm(out, kdT[chunk_rows(c), c // 2, :], vg_tok[chunk_rows(c), c // 2, :], start=True, stop=True)

                for t in range(MIX_N):
                    pe.wait_ge(result_read, rb + (t - 1 + CREDIT_RES))
                    tile(tb, t, x_hi, x_lo, chunk_wait=xc if t == 0 else None)
                    if t == 4:
                        pe.wait_ge(gla_qk_ready, v)
                        transposes(X[0], E[:, NL, :], 0).then_inc(k_trans, 1)
                        pe.wait_ge(rope_ready, at(2, 1))
                        for h in range(2):
                            transposes(X[1 + h], kr[:, h, :], 0).then_inc(k_trans, 1)
                        pe.wait_ge(k_raw_in, 16 * v)
                        for h in range(2):
                            for i in range(2):
                                last = nc.tensor.transpose(X[3][:, (2 * h + i) * P:(2 * h + i + 1) * P],
                                                           k_raw[:, i, h * P:(h + 1) * P], ident)
                        last.then_inc(k_trans, 1)
                    if t == 6:
                        pe.wait_ge(rope_ready, 2 * v)
                        pe.wait_ge(k_copied, 7 * v)
                        scores(0)
                    if t == 7:
                        for pair in range(3):
                            for c in range(2 * pair, min(2 * pair + 2, NCH)):
                                cols = slice(c * CH, (c + 1) * CH)
                                for lev in range(NL + 1):
                                    lhs = E[:, lev, cols] if lev < NL else kg[:, cols]
                                    rhs = E[:, lev, cols] if lev < NL else qg[:, cols]
                                    last = mm(X[1 + pair][chunk_rows(c), lev * CH:(lev + 1) * CH], lhs, rhs, start=True, stop=True)
                            last.then_inc(pairs_done, 1)
                    if t == 9:
                        pe.wait_ge(a_ready, 3 * v)
                        for e in range(2):
                            transposes(X[1 + e], vgT[:, e, :], 0).then_inc(vg_trans, 1)
                        att_transposes(0)
                    if t == 10:
                        pe.wait_ge(vg_copied, 4 * v)
                        pe.wait_ge(result_read, rb + (10 + CREDIT_RES))
                        for h in range(2):
                            transposes(X[1 + h], vz[:, h, :], 0).then_inc(v_trans, 1)
                        pe.wait_ge(att_copied, at(6, 3))
                        scores(1)
                    if t == 11:
                        own_sum(0, X[3][:, 0:GDV])
                        own_sum(2, X[3][:, GDV:2 * GDV]).then_inc(u_done, 1)
                    if t == 12:
                        pe.wait_ge(v_copied, 4 * v)
                        pe.wait_ge(v_past_in, 16 * v)
                        values(0, X[1])
                        own_sum(1, X[2][:, 0:GDV])
                        own_sum(3, X[2][:, GDV:2 * GDV]).then_inc(u_done, 1)
                    if t == 13:
                        att_transposes(1)
                        own_sum(4, X[5][:, 0:GDV]).then_inc(u_done, 1)
                    if t == 14:
                        pe.wait_ge(state_ready, at(5, 4))
                        for parity, e in ((0, 0), (0, 1), (1, 0), (1, 1)):
                            if parity:
                                pe.wait_ge(og_even, at(2, e + 1))
                            for c in range(parity, NCH, 2):
                                out = X[2 + e][:, c * CH:(c + 1) * CH]
                                ec = slice(e * P, (e + 1) * P)
                                old = None if c == 0 else (S[:, c - 1, ec] if c < NCH - 1 else s_past[:, ec])
                                if old is not None:
                                    if c == NCH - 1:
                                        pe.wait_ge(s_past_in, 16 * v)
                                    mm(out, old, E[:, NL + 1, c * CH:(c + 1) * CH], start=True, stop=False)
                                last = mm(out, vg_tok[chunk_rows(c), c // 2, ec], a_sum[chunk_rows(c), c // 2, :],
                                          start=old is None, stop=True)
                            last.then_inc(og_done if parity else og_even, 1)
                        pe.wait_ge(o_squared, at(4, 2))
                        mm(X[1][:, 0:T], ones, o_sq[:, :], start=True, stop=True).then_inc(o_sum, 1)
                    if t == 15:
                        values(1, X[0])
                        pe.wait_ge(o_rstd, at(2, 1))
                        pe.wait_ge(og_squared, 2 * v)
                        for e in range(2):
                            last = mm(X[1][:, 0:T], ones, og_q[:, e, :], start=e == 0, stop=e == 1)
                        last.then_inc(og_sum, 1)
                        pe.wait_ge(state_ready, 5 * v)
                        pe.wait_ge(o_squared, 4 * v)
                        mm(X[5][:, 0:T], ones, o_sq[:, :], start=True, stop=True).then_inc(o_sum, 1)

            wait_plain(pe, consts_in, blo_ready, l * (2 * KC) + KC)
            with pe.Fori(0, MRG_IT) as j:
                tb = pe.snap(l * TILES + j * MRG_N + MRG_0)
                rb = pe.snap(l * RESULTS + j * MRG_N + RES_MRG)
                for t in range(MRG_N):
                    if t == 2:
                        pe.wait_ge(blo_ready, l * (2 * KC) + 2 * KC)
                    pe.wait_ge(result_read, rb + (t - 1 + CREDIT_RES))
                    tile(tb, t, b_hi, b_lo, k0=KC if t < 2 else 0)
            with pe.Fori(0, OUT_IT) as j:
                tb = pe.snap(l * TILES + j * OUT_N + OUT_0)
                for t in range(OUT_N):
                    if t == 0:
                        pe.wait_ge(mixlo_ready, l * MRG_IT + MRG_IT)
                    pe.wait_ge(x_ready, l * 24 + j * 4 + (8 + t - 1))
                    tile(tb, t, x_hi, x_lo)

            pe.wait_ge(xlo_ready, l * 24 + 9)
            norm_sums(l * 3 + 2)
            with pe.Fori(0, FUP_IT) as j:
                tb = pe.snap(l * TILES + j * FUP_N + FUP_0)
                rb = pe.snap(l * RESULTS + j * FUP_N + RES_FUP)
                xc = pe.snap(l * 24 + 8)
                for t in range(FUP_N):
                    pe.wait_ge(result_read, rb + (t - 1 + CREDIT_RES))
                    tile(tb, t, x_hi, x_lo, chunk_wait=xc if t == 0 else None)
            pe.wait_ge(pe_in, l * 32 + 32)
            for c in range(2):
                for i in range(3):
                    n = rows(i)
                    last = nc.tensor.transpose(X[3 + c][:, i * P:i * P + n], pe_tok[0:n, i, c * P:(c + 1) * P], ident[0:n, 0:n])
                last.then_inc(pe_trans, 1)
            with pe.Fori(0, FDN_IT) as j:
                tb = pe.snap(l * TILES + j * FDN_N + FDN_0)
                for t in range(FDN_N):
                    pair, k, mt = t // 6, t // 2 % 3, t % 2
                    if k == 0:
                        pe.wait_ge(result_read, l * RESULTS + (RESULTS - 1 + mt + CREDIT_RES))
                        pe.wait_ge(x_ready, l * 24 + j * 4 + (16 + 2 * pair + mt - 1))
                    if mt == 0:
                        pe.wait_ge(hlo_ready, l * FUP_IT + (4, 8, 11)[k])
                    tile(tb, t, h_hi, h_lo, k0=KC * k, nk=FDN_K[k], start=k == 0, stop=k == 2)

            pe.wait_ge(xlo_ready, l * 24 + 17)
            norm_sums(l * 3 + 3)
            wait_plain(pe, consts_in, peT_ready, l * 2 + 2)
            with pe.Fori(0, PLE_IT) as j:
                tb = pe.snap(l * TILES + j * PLE_N + PLE_0)
                n8 = pe.snap(l * KC + j * PLE_N)
                xc = pe.snap(l * 24 + 16)
                for t in range(PLE_N):
                    if t % 2 == 0:
                        pe.wait_ge(wple_in[t // 2], l * (16 * PLE_IT) + j * 16 + 16)
                    pe.wait_ge(ple_used, n8 + (t + 1))
                    for c in range(2):
                        last = mm(X[1 + t % 2][:, 0:T], wple[:, t // 2, c, t % 2 * P:(t % 2 + 1) * P], peT[:, c, :],
                                  start=c == 0, stop=c == 1)
                    last.then_inc(ple_done, 1)
                    pe.wait_ge(gz_ready, n8 + (t + 1))
                    tile(tb, t, x_hi, x_lo, chunk_wait=xc if t == 0 else None)

        norm_sums(3 * DEPTH + 1)
        pe.wait_ge(y_ready, KC)
        for t in range(3):
            for half in range(2):
                for m in range(4):
                    c = 4 * half + m
                    last = nc.tensor.transpose(X[2 * t + half][0:rows(t), m * P:(m + 1) * P], xT[:, c, t * P:t * P + rows(t)], ident)
                last.then_inc(y_trans, 1)

    ctx.close()


OUTS = [("y_prompt", (1, TP, D)), ("y_sample", (1, TS, D)),
        ("k_prompt", (DEPTH, 1, TP, HEADS, DV)), ("v_prompt", (DEPTH, 1, TP, HEADS, DV)),
        ("s_prompt", (DEPTH, 1, GH, GDK, GDV)),
        ("k_sample", (DEPTH, 1, TS, HEADS, DV)), ("v_sample", (DEPTH, 1, TS, HEADS, DV)),
        ("s_sample", (DEPTH, 1, GH, GDK, GDV))]


def constants():
    import math

    import numpy as np
    f = np.float32
    c = np.zeros((P, NCONST), f)
    c[:, K_ID:K_ID + P] = np.eye(P)
    c[:, K_ONE:K_ONE + P] = 1.0
    half = DH // 8
    inv = f(500000.0) ** (-np.arange(0, 2 * half, 2, dtype=f) / f(2 * half))
    ang = np.arange(T, dtype=f)[None, :] * inv[:, None]
    c[:, K_COS:K_COS + T] = 1.0
    for m in range(2):
        for i in range(half):
            a, b = m * DH + i, m * DH + half + i
            c[a, K_COS:K_COS + T] = c[b, K_COS:K_COS + T] = np.cos(ang[i])
            c[a, K_SIN:K_SIN + T] = -np.sin(ang[i])
            c[b, K_SIN:K_SIN + T] = np.sin(ang[i])
    c[:, K_RST:K_RST + T] = np.arange(T) % CH != 0
    k, q = np.arange(CH)[:, None], np.arange(CH)[None, :]
    for lev, h in enumerate(LEVELS + [0]):
        ok = (k == q) if h == 0 else (k // (2 * h) == q // (2 * h)) & (k % (2 * h) < h) & (q % (2 * h) >= h)
        c[:, K_MASK + lev * CH:K_MASK + (lev + 1) * CH] = np.concatenate([ok, ok])
    c[:, K_ID2:K_ID2 + TS] = np.concatenate([np.eye(TS)] * 2)
    c[0, K_MQ:K_MQ + CH] = -1e30
    c[:, K_EPS] = EPS
    low = np.arange(P) < DH
    c[:, K_A5:K_A5 + 5] = np.array([1, 0, 1, 0, 0], f)
    c[:, K_B5:K_B5 + 5] = np.array([0, 1, 0, 1, 0], f)
    c[:, K_A5 + 4], c[:, K_B5 + 4] = low, ~low
    for l in range(DEPTH):
        li = 0.8 - 0.6 * math.exp(-0.3 * l)
        c[:, K_LI + l], c[:, K_OM + l] = li, 1.0 - li
    return c


def kernel(**inputs):
    import numpy as np
    import concourse.bacc as bacc
    from concourse.bass_utils import run_bass_kernel_spmd

    nc = bacc.Bacc("TRN2", target_bir_lowering=False, num_devices=1)
    arrays, A, O = {}, {}, {}
    for name, a in list(inputs.items()) + [("consts", constants())]:
        a = np.ascontiguousarray(a)
        arrays[f"in_{name}"] = a
        A[name] = nc.dram_tensor(f"in_{name}", a.shape, F32, kind="ExternalInput").ap()
    for name, shape in OUTS:
        O[name] = nc.dram_tensor(f"out_{name}", shape, F32, kind="ExternalOutput").ap()
    encoder(nc, A, O)
    r = run_bass_kernel_spmd(nc, [arrays], core_ids=[0])
    return tuple(r.results[0][f"out_{name}"] for name, _ in OUTS)
```

```python
from contextlib import ExitStack

import concourse.bass as bass
from concourse import mybir

F32 = mybir.dt.float32
F32R = mybir.dt.float32r
ALU = mybir.AluOpType
ACT = mybir.ActivationFunctionType
AX = mybir.AxisListType

P = 128
DEPTH = 2
D = 1024
KC = D // P
TP, TS = 256, 64
T = TP + TS
PAST = 256
HEADS, DH, DV = 8, 64, 128
GH, GDK, GDV, RANK = 4, 128, 256, 16
CH = 64
NCH = T // CH
FF = 2816
FC = FF // P
PLE = 256
EPS = 1e-6
LEVELS = [32, 16, 8, 4, 2, 1]
NL = len(LEVELS)
UW = 256

C_Q, C_K, C_V = 0, 1024, 2048
C_QG, C_KG, C_VG, C_RG = 3072, 3584, 4096, 5120
C_AG, C_GA, C_GB = 6144, 6160, 7184

MIX_IT, MIX_N = 4, 16
MRG_IT, MRG_N = 4, 4
OUT_IT, OUT_N = 2, 4
FUP_IT, FUP_N = 11, 4
FDN_IT, FDN_N = 2, 12
PLE_IT, PLE_N = 2, 4
MRG_0 = MIX_IT * MIX_N
OUT_0 = MRG_0 + MRG_IT * MRG_N
FUP_0 = OUT_0 + OUT_IT * OUT_N
FDN_0 = FUP_0 + FUP_IT * FUP_N
PLE_0 = FDN_0 + FDN_IT * FDN_N
TILES = PLE_0 + PLE_IT * PLE_N
RES_MRG = MRG_0
RES_FUP = RES_MRG + MRG_IT * MRG_N
RESULTS = RES_FUP + FUP_IT * FUP_N
FDN_K = [8, 8, 6]
CREDIT_TILE = 4
CREDIT_RES = 2

K_ID, K_ONE, K_EPS = 0, 128, 256
K_A5 = K_EPS + 1
K_B5 = K_A5 + 5
K_LI = K_B5 + 5
K_GS = K_LI + DEPTH
NPAR = 70
K_COS = K_GS + NPAR
K_SIN, K_RST, K_MASK = K_COS + T, K_COS + 2 * T, K_COS + 3 * T
K_ID2 = K_MASK + (NL + 1) * CH
K_MQ = K_ID2 + 64
NCONST = K_MQ + 128

R_MIX, R_FFN, R_PLE, R_FIN, R_SUB, R_GN, R_BG = 0, 16, 32, 48, 56, 58, 62
U_MIX, U_FFN, U_PLE, U_SUB, U_GN, U_BG, U_C5 = 0, 8, 16, 24, 25, 27, 31
NCUR = 36

SWAP = [8 + i for i in range(8)] + list(range(8)) + list(range(16, 32))


def wait_plain(eng, known, sem, value):
    value = eng.to_reg(value)
    eng.wait_ge(known, 16)
    eng.wait_ge(sem, value)


SIGMOID, LN_EXP, SILU = 2, 6, 18


class Steps:

    def __init__(self, eng, sem, base, total):
        self.eng, self.sem, self.base, self.total, self.n = eng, sem, base, total, 0

    def put(self, ins):
        self.n += 1
        ins.then_inc(self.sem, 1)

    def wait(self):
        self.eng.wait_ge(self.sem, self.base + self.n)

    def close(self):
        assert self.n == self.total, (self.n, self.total)


def encoder(nc, A, O):
    w_in = A["w_in"].rearrange("l (c p) n -> p (l c) n", p=P)
    w_pa = A["w_pa"].rearrange("l (c p) n -> p (l c) n", p=P)
    w_pb = A["w_pb"].rearrange("l (c p) n -> p (l c) n", p=P)
    w_o = A["w_o"].rearrange("l (c p) n -> p (l c) n", p=P)
    w_f1 = A["w_f1"].rearrange("l (c p) n -> p (l c) n", p=P)
    w_f3 = A["w_f3"].rearrange("l (c p) n -> p (l c) n", p=P)
    w_f2 = A["w_f2"].rearrange("l (c p) n -> p (l c) n", p=P)
    w_gate = A["w_ple_gate"].rearrange("l (c p) n -> p (l c) n", p=P)
    w_ple = A["w_ple"].rearrange("l (c p) n -> p (l c) n", p=P)
    w_ga2 = A["w_ga2"].rearrange("l r n -> r l n")
    cache_k = A["cache_k"].rearrange("l b (c p) h e -> p (l b c) (h e)", p=P)
    cache_v = A["cache_v"].rearrange("l b (c p) h e -> p (l b c) (h e)", p=P)
    state_in = A["state_gla"].rearrange("l b h d e -> d (l b h) e")
    pe_p = A["p_prompt"].rearrange("l b (c p) n -> p (l b c) n", p=P)
    pe_s = A["p_sample"].rearrange("l b t n -> t (l b) n")
    x_p = A["x_prompt"].rearrange("b (c p) d -> p (b c) d", p=P)
    x_s = A["x_sample"].rearrange("b t d -> t (b d)")
    y_p = O["y_prompt"].rearrange("b (c p) d -> p (b c) d", p=P)
    y_s = O["y_sample"].rearrange("b t d -> t (b d)")
    kv_p = [O[n].rearrange("l b (c p) h e -> p (l b c) (h e)", p=P) for n in ("k_prompt", "v_prompt")]
    kv_s = [O[n].rearrange("l b t h e -> t (l b) (h e)") for n in ("k_sample", "v_sample")]
    st_p = O["s_prompt"].rearrange("l b h d e -> d (l b h) e")
    st_s = O["s_sample"].rearrange("l b h d e -> d (l b h) e")

    ctx = ExitStack()

    def sb(name, shape, dt=F32, where=ctx):
        return where.enter_context(nc.sbuf_tensor(name, shape, dt))

    def sem(name):
        return ctx.enter_context(nc.semaphore(name))

    xT = sb("xT", [P, KC, T])
    x_hi = sb("x_hi", [P, KC, T], F32R)
    x_lo = sb("x_lo", [P, KC, T], F32R)
    w_raw = sb("w_raw", [P, 2, KC, UW])
    w_hi = sb("w_hi", [P, 4, KC, P], F32R)
    w_lo = sb("w_lo", [P, 4, KC, P], F32R)
    cst = sb("cst", [P, NCONST])
    parT = sb("parT", [P, NPAR])
    c5 = sb("c5", [P, DEPTH, 5])
    cur = sb("cur", [P, NCUR])
    ssq = sb("ssq", [P, T])
    sqt = sb("sqt", [P, T])
    rstd = sb("rstd", [P, T])
    agT = sb("agT", [RANK, T])
    w_ag = sb("w_ag", [P, KC, RANK])
    w_agg = sb("w_agg", [P, KC, RANK])
    ga2 = sb("ga2", [RANK, GH * GDK])

    with ExitStack() as where:
        k_raw = sb("k_raw", [P, 2, UW], where=where)
        v_past = sb("v_past", [P, 2, UW], where=where)
        s_past = sb("s_past", [P, GDV], where=where)
        E = sb("E", [P, NL + 2, T], where=where)
        ebl = sb("ebl", [P, NCH], where=where)
        qg = sb("qg", [P, T], where=where)
        kg = sb("kg", [P, T], where=where)
        kdT = sb("kdT", [P, 3, P], where=where)
        vgT = sb("vgT", [P, 2, T], where=where)
        vg_tok = sb("vg_tok", [P, 3, GDV], where=where)
        a_msk = sb("a_msk", [P, NL + 1, CH], where=where)
        a_sum = sb("a_sum", [P, 3, CH], where=where)
        z = sb("z", [P, 2, T], where=where)
        rot = sb("rot", [P, 2, T], where=where)
        kr = sb("kr", [P, 2, T], where=where)
        qr = sb("qr", [P, 2, T], where=where)
        vz = sb("vz", [P, 2, T], where=where)
        kcT = sb("kcT", [P, 2, PAST], where=where)
        mx = sb("mx", [P, 5], where=where)
        nb = sb("nb", [P, 5], where=where)
        sums = sb("sums", [P, 5], where=where)
        coef = sb("coef", [P, 5], where=where)
        p0 = sb("p0", [P, 2, P], where=where)
        p1 = sb("p1", [P, 2, 2 * P], where=where)
        p_s = sb("p_s", [P, PAST + TS], where=where)
        dmat = sb("dmat", [P, TS], where=where)
        attT = sb("attT", [P, 576], where=where)
        o_sq = sb("o_sq", [P, T], where=where)
        rs = sb("rs", [P, 3, T], where=where)
        zg = sb("zg", [P, GH, T], where=where)
        k_tok = sb("k_tok", [P, 3, UW], where=where)
        v_tok = sb("v_tok", [P, 3, UW], where=where)
        S = sb("S", [P, 4, GDV], where=where)
        S_smp = sb("S_smp", [P, GDV], where=where)
        gab = sb("gab", [P, 2 * KC, T], where=where)
        oag = sb("oag", [P, 2 * KC, T], where=where)
    o_sb, zr, og_t, sig, og_q = vz, vgT, z, rot, qr
    mix_hi, mix_lo = oag[:, 0:KC, :].bitcast(F32R), oag[:, KC:2 * KC, :].bitcast(F32R)
    lg = gab[:, 2 * KC - GH:2 * KC, :]
    with ExitStack() as where:
        a_hi = sb("a_hi", [P, KC, T], F32R, where=where)
        a_lo = sb("a_lo", [P, KC, T], F32R, where=where)
        m1 = sb("m1", [P, 2, T], where=where)
        m2 = sb("m2", [P, 2, T], where=where)
    with ExitStack() as where:
        h_hi = sb("h_hi", [P, FC, T], F32R, where=where)
        h_lo = sb("h_lo", [P, FC, T], F32R, where=where)
        f1z = sb("f1z", [P, 2, T], where=where)
        f3z = sb("f3z", [P, 2, T], where=where)
        gz = sb("gz", [P, T], where=where)
        gs = sb("gs", [P, T], where=where)
        pe_tok = sb("pe_tok", [P, 3, PLE], where=where)
        wple = sb("wple", [P, 2, 2, UW], where=where)
        peT = sb("peT", [P, 2, T], where=where)
    with ExitStack() as where:
        x_tok = sb("x_tok", [P, 3, D], where=where)
        par = sb("par", [NPAR, P], where=where)
        lrow = sb("lrow", [1, 4, DEPTH * DH], where=where)
        lprod = sb("lprod", [1, 2, DEPTH * DH], where=where)
        lsum = sb("lsum", [1, 2, DEPTH], where=where)
        lexp = sb("lexp", [1, 2, DEPTH], where=where)
        lneg = sb("lneg", [1, DEPTH], where=where)
        nlam = sb("nlam", [P, DEPTH], where=where)

    big = [ctx.enter_context(nc.psum_tensor(f"big{i}", [P, 512], F32)) for i in range(2)]
    X = [ctx.enter_context(nc.psum_tensor(f"X{i}", [P, 512], F32)) for i in range(6)]

    raw_in = [sem("raw_in0"), sem("raw_in1")]
    consts_in = sem("consts_in")
    tables_in = sem("tables_in")
    par_in = sem("par_in")
    x_in = [sem("x_in0"), sem("x_in1")]
    lam_in = sem("lam_in")
    ag_in = sem("ag_in")
    k_raw_in = sem("k_raw_in")
    v_past_in = sem("v_past_in")
    s_past_in = sem("s_past_in")
    pe_in = sem("pe_in")
    wple_in = [sem("wple_in0"), sem("wple_in1")]
    stores_left = sem("stores_left")
    k_stored = sem("k_stored")
    v_stored = sem("v_stored")
    s_stored = sem("s_stored")
    y_stored = sem("y_stored")
    hi_ready = sem("hi_ready")
    lo_ready = sem("lo_ready")
    tile_done = sem("tile_done")
    result_read = sem("result_read")
    x_ready = sem("x_ready")
    ssq_ready = sem("ssq_ready")
    norm_sum = sem("norm_sum")
    rstd_ready = sem("rstd_ready")
    xhi_ready = sem("xhi_ready")
    xlo_ready = sem("xlo_ready")
    cur_ready = sem("cur_ready")
    agg_ready = sem("agg_ready")
    ag_done = sem("ag_done")
    agT_ready = sem("agT_ready")
    g_done = sem("g_done")
    zg_ready = sem("zg_ready")
    lg_ready = sem("lg_ready")
    bcur_ready = sem("bcur_ready")
    args_ready = sem("args_ready")
    decay_ready = sem("decay_ready")
    gla_qk_ready = sem("gla_qk_ready")
    vg_trans = sem("vg_trans")
    vg_copied = sem("vg_copied")
    u_done = sem("u_done")
    state_ready = sem("state_ready")
    pairs_done = sem("pairs_done")
    a_ready = sem("a_ready")
    og_done = sem("og_done")
    og_even = sem("og_even")
    og_squared = sem("og_squared")
    og_sum = sem("og_sum")
    og_rstd = sem("og_rstd")
    sig_ready = sem("sig_ready")
    shuffled = sem("shuffled")
    sin_ready = sem("sin_ready")
    rope_ready = sem("rope_ready")
    k_trans = sem("k_trans")
    k_copied = sem("k_copied")
    v_trans = sem("v_trans")
    v_copied = sem("v_copied")
    scores_done = sem("scores_done")
    negmax_ready = sem("negmax_ready")
    probs_ready = sem("probs_ready")
    maps_ready = sem("maps_ready")
    att_trans = sem("att_trans")
    att_copied = sem("att_copied")
    pv_done = sem("pv_done")
    o_squared = sem("o_squared")
    o_sum = sem("o_sum")
    o_rstd = sem("o_rstd")
    branch_ready = sem("branch_ready")
    gates_ready = sem("gates_ready")
    bhi_ready = sem("bhi_ready")
    blo_ready = sem("blo_ready")
    mixed_ready = sem("mixed_ready")
    mixhi_ready = sem("mixhi_ready")
    mixlo_ready = sem("mixlo_ready")
    silu_ready = sem("silu_ready")
    h_ready = sem("h_ready")
    hhi_ready = sem("hhi_ready")
    hlo_ready = sem("hlo_ready")
    pe_trans = sem("pe_trans")
    peT_ready = sem("peT_ready")
    ple_done = sem("ple_done")
    ple_used = sem("ple_used")
    gz_ready = sem("gz_ready")
    gs_ready = sem("gs_ready")
    par_trans = sem("par_trans")
    x_trans = sem("x_trans")
    lsum_ready = sem("lsum_ready")
    lexp_ready = sem("lexp_ready")
    lneg_ready = sem("lneg_ready")
    lam_bc = sem("lam_bc")
    y_ready = sem("y_ready")
    y_trans = sem("y_trans")
    y_copied = [sem("y_copied_dve"), sem("y_copied_act")]
    dve_pro, dve_mix = sem("dve_pro"), sem("dve_mix")
    act_rms, act_decay, act_mix, act_gate = sem("act_rms"), sem("act_decay"), sem("act_mix"), sem("act_gate")
    pool_sq, pool_acc = sem("pool_sq"), sem("pool_acc")

    ident = cst[:, K_ID:K_ID + P]
    ones = cst[:, K_ONE:K_ONE + P]
    cos2 = cst[:, None, K_COS:K_COS + T].broadcast_to([P, 2, T])
    sin2 = cst[:, None, K_SIN:K_SIN + T].broadcast_to([P, 2, T])
    amask = cst[:, K_MASK:K_MASK + (NL + 1) * CH].rearrange("p (a b) -> p a b", a=NL + 1)

    def bc(ap, shape):
        return ap.broadcast_to(shape)

    def rows(tile):
        return TS if tile == 2 else P

    def halves(ap, h):
        v = ap.rearrange("p (n a h) -> p n a h", a=2, h=h)
        return v[:, :, 0, :], v[:, :, 1, :]

    block = ctx.enter_context(nc.Block())

    @block.sync
    def _(sp):
        for half in range(2):
            c = slice(half * (D // 2), (half + 1) * (D // 2))
            sp.dma_start(x_tok[:, 0:2, c], x_p[:, :, c]).then_inc(x_in[half], 16)
            sp.dma_start(x_tok[0:TS, 2, c], x_s[:, c]).then_inc(x_in[half], 16)

        def unit(tb, c, src, row0, nrow, col0):
            sp.wait_ge(lo_ready, tb + (2 * c + CREDIT_TILE - 2))
            for r in range(0, nrow, nrow // 2):
                sp.dma_start(w_raw[:, c % 2, r:r + nrow // 2, :],
                             src[:, bass.ds(row0 + r, nrow // 2), bass.ds(col0, UW)]).then_inc(raw_in[c % 2], 16)

        def qk_unit(tb, l, j):
            sp.wait_ge(lo_ready, tb + (CREDIT_TILE - 2))
            for half, col in enumerate((C_QG, C_KG)):
                sp.dma_start(w_raw[:, 0, :, half * P:(half + 1) * P],
                             w_in[:, bass.ds(l * KC, KC), bass.ds(j * P + col, P)]).then_inc(raw_in[0], 16)

        with sp.Fori(0, DEPTH) as l:
            sp.dma_start(w_ag[:, :, :], w_in[:, bass.ds(l * KC, KC), C_AG:C_AG + RANK]).then_inc(ag_in, 16)
            sp.dma_start(ga2[:, None, :], w_ga2[:, bass.ds(l, 1), :]).then_inc(ag_in, 16)
            with sp.Fori(0, MIX_IT) as j:
                tb = sp.snap(l * TILES + j * MIX_N)
                qk_unit(tb, l, j)
                unit(tb, 1, w_in, l * KC, KC, j * UW + C_K)
                sp.wait_ge(x_trans, KC)
                sp.dma_start(k_raw[:, :, :], cache_k[:, bass.ds(l * 2, 2), bass.ds(j * UW, UW)]).then_inc(k_raw_in, 16)
                unit(tb, 2, w_in, l * KC, KC, j * UW + C_Q)
                unit(tb, 3, w_in, l * KC, KC, j * UW + C_VG)
                unit(tb, 4, w_in, l * KC, KC, j * UW + C_V)
                sp.dma_start(v_past[:, :, :], cache_v[:, bass.ds(l * 2, 2), bass.ds(j * UW, UW)]).then_inc(v_past_in, 16)
                sp.dma_start(s_past[:, None, :], state_in[:, bass.ds(l * GH + j, 1), :]).then_inc(s_past_in, 16)
                unit(tb, 5, w_in, l * KC, KC, j * UW + C_RG)
                unit(tb, 6, w_in, l * KC, KC, j * UW + C_GA)
                unit(tb, 7, w_in, l * KC, KC, j * UW + C_GB)
            with sp.Fori(0, MRG_IT) as j:
                tb = sp.snap(l * TILES + j * MRG_N + MRG_0)
                unit(tb, 0, w_pb, l * KC, KC, j * UW)
                unit(tb, 1, w_pa, l * KC, KC, j * UW)
            with sp.Fori(0, OUT_IT) as j:
                tb = sp.snap(l * TILES + j * OUT_N + OUT_0)
                unit(tb, 0, w_o, l * KC, KC, j * (2 * UW))
                unit(tb, 1, w_o, l * KC, KC, j * (2 * UW) + UW)
            with sp.Fori(0, FUP_IT) as j:
                tb = sp.snap(l * TILES + j * FUP_N + FUP_0)
                unit(tb, 0, w_f1, l * KC, KC, j * UW)
                unit(tb, 1, w_f3, l * KC, KC, j * UW)
            sp.wait_ge(stores_left, l * MIX_IT + (MIX_IT + 1))
            sp.dma_start(pe_tok[:, 0:2, :], pe_p[:, bass.ds(l * 2, 2), :]).then_inc(pe_in, 16)
            sp.dma_start(pe_tok[0:TS, 2:3, :], pe_s[:, bass.ds(l, 1), :]).then_inc(pe_in, 16)
            with sp.Fori(0, FDN_IT) as j:
                tb = sp.snap(l * TILES + j * FDN_N + FDN_0)
                for pair in range(2):
                    for k, nk in enumerate(FDN_K):
                        unit(tb, 3 * pair + k, w_f2, l * FC + KC * k, nk, j * (2 * UW) + pair * UW)
            with sp.Fori(0, PLE_IT) as j:
                tb = sp.snap(l * TILES + j * PLE_N + PLE_0)
                for c in range(2):
                    unit(tb, c, w_gate, l * KC, KC, j * (2 * UW) + c * UW)
                    sp.wait_ge(tile_done, tb + (2 * c + CREDIT_TILE - 2))
                    sp.dma_start(wple[:, c, :, :], w_ple[:, bass.ds(l * 2, 2),
                                                         bass.ds(j * (2 * UW) + c * UW, UW)]).then_inc(wple_in[c], 16)
        sp.wait_ge(lo_ready, DEPTH * TILES + CREDIT_TILE - 2)
        for r in range(0, KC, KC // 2):
            sp.dma_start(w_raw[:, 0, r:r + KC // 2, :], w_in[:, r:r + KC // 2, 0:UW]).then_inc(raw_in[0], 16)
        for t in range(3):
            sp.wait_ge(y_copied[0], t + 1)
            sp.wait_ge(y_copied[1], t + 1)
            dst = y_p[:, t, :] if t < 2 else y_s[:, :]
            sp.dma_start(dst, x_tok[0:rows(t), t, :]).then_inc(y_stored, 16)
        sp.wait_ge(y_stored, 48)

    @block.gpsimd
    def _(pool):
        for n, key in enumerate(("lambda_q1", "lambda_k1", "lambda_q2", "lambda_k2")):
            pool.dma_start(lrow[:, n, :], A[key].rearrange("(a l) d -> a (l d)", a=1)).then_inc(lam_in, 16)
        pool.sem_inc(stores_left, 1)

        def clear_ssq(sums_seen):
            if sums_seen is not None:
                wait_plain(pool, consts_in, norm_sum, sums_seen)
            nc.gpsimd.memset(ssq[:, :], 0.0).then_inc(pool_acc, 1)

        def square(n, chunk):
            pool.wait_ge(pool_acc, n[1])
            wait_plain(pool, consts_in, x_ready, n[0] + 1)
            nc.gpsimd.tensor_tensor(sqt[:, None, :], xT[:, chunk, :], xT[:, chunk, :], ALU.mult).then_inc(pool_sq, 1)
            pool.wait_ge(pool_sq, n[0] + 1)
            nc.gpsimd.tensor_tensor(ssq[:, :], ssq[:, :], sqt[:, :], ALU.add).then_inc(pool_acc if n[2] else ssq_ready, 1)

        clear_ssq(None)
        for c in range(KC):
            square((c, c + 1, c < KC - 1), slice(c, c + 1))

        def squares_of_loop(l, norm, iters, per):
            clear_ssq(l * 3 + norm)
            with pool.Fori(0, iters - 1) as j:
                for t in range(per):
                    n = pool.snap(l * 24 + j * per + (8 * norm + t))
                    a = pool.snap(l * 24 + j * per + (8 * norm + t + 1))
                    square((n, a, True), bass.ds(j * per + t, 1))
            for t in range(per):
                c = (iters - 1) * per + t
                n = pool.snap(l * 24 + (8 * norm + c))
                square((n, n + 1, c < KC - 1), slice(c, c + 1))

        pool.wait_ge(tables_in, 16)
        with pool.Fori(0, DEPTH) as l:
            with pool.Fori(0, MIX_IT) as j:
                v = pool.snap(l * MIX_IT + j + 1)
                k_count, v_count = pool.snap(v * 7 - 3), pool.snap(v * 4)
                b = E[:, NL + 1, :]
                pool.wait_ge(bcur_ready, v)
                for lev, h in enumerate(LEVELS):
                    first, second = halves(b, h)
                    o1, o2 = halves(E[:, lev, :], h)
                    ref = bc(first[:, :, h - 1:h], [P, T // (2 * h), h])
                    nc.gpsimd.tensor_tensor(o1, ref, first, ALU.subtract).then_inc(args_ready, 1)
                    nc.gpsimd.tensor_tensor(o2, second, ref, ALU.subtract).then_inc(args_ready, 1)
                bch = b.rearrange("p (n c) -> p n c", c=CH)
                nc.gpsimd.tensor_tensor(E[:, NL, :].rearrange("p (n c) -> p n c", c=CH),
                                        bc(bch[:, :, CH - 1:CH], [P, NCH, CH]), bch, ALU.subtract).then_inc(args_ready, 1)
                for n in range(2):
                    pool.wait_ge(shuffled, 2 * v + (n - 1))
                    nc.gpsimd.tensor_tensor(rot[:, :, :], rot[:, :, :], sin2, ALU.mult).then_inc(sin_ready, 1)
                for tok, copied, count, stored, which in ((k_tok, k_copied, k_count, k_stored, 0), (v_tok, v_copied, v_count, v_stored, 1)):
                    wait_plain(pool, consts_in, copied, count)
                    pool.dma_start(kv_p[which][:, bass.ds(l * 2, 2), bass.ds(j * UW, UW)], tok[:, 0:2, :]).then_inc(stored, 16)
                    pool.dma_start(kv_s[which][:, bass.ds(l, 1), bass.ds(j * UW, UW)], tok[0:TS, 2:3, :]).then_inc(stored, 16)
                wait_plain(pool, consts_in, state_ready, 5 * v)
                pool.dma_start(st_p[:, bass.ds(l * GH + j, 1), :], S[:, 3:4, :]).then_inc(s_stored, 16)
                pool.dma_start(st_s[:, bass.ds(l * GH + j, 1), :], S_smp[:, None, :]).then_inc(s_stored, 16)
                for stored in (k_stored, v_stored, s_stored):
                    pool.wait_ge(stored, v * 32)
                pool.sem_inc(stores_left, 1)
            squares_of_loop(l, 1, OUT_IT, 4)
            squares_of_loop(l, 2, FDN_IT, 4)
            squares_of_loop(l, 3, PLE_IT, 4)
        for stored in (k_stored, v_stored, s_stored):
            pool.wait_ge(stored, 32 * MIX_IT * DEPTH)

    @block.scalar
    def _(act):
        def hi(tb, tb8, t, nk):
            act.wait_ge(raw_in[(t // 2) % 2], tb8 + 32 * (t // 4 + 1))
            act.wait_ge(tile_done, tb + (t + 1))
            nc.scalar.copy(w_hi[:, t % 4, 0:nk, :], w_raw[:, (t // 2) % 2, 0:nk, (t % 2) * P:(t % 2 + 1) * P]).then_inc(hi_ready, 1)

        def base(l, j, per, first):
            return act.snap(l * TILES + j * per + first), act.snap(l * (8 * TILES) + j * (8 * per) + 8 * first)

        def tables(which):
            act.add_instruction(mybir.InstLoadActFuncSet(name=nc.get_next_instruction_name(), ins=[], outs=[], act_func_set_id=which))

        def rms(out, src, scale, done, steps, arrived, count):
            act.wait_ge(arrived, count)
            steps.put(nc.scalar.activation(out, src[:, 0:T], ACT.Ln, scale=scale, bias=cst[:, K_EPS:K_EPS + 1]))
            steps.wait()
            nc.scalar.activation(out, out, ACT.Exp, scale=-0.5).then_inc(done, 1)

        def sigmoid(x, seen, count):
            for n in range(3):
                if n:
                    wait_plain(act, consts_in, seen, count + n)
                ins = nc.scalar.activation(x, x, ACT.Ln if n == 1 else ACT.Exp, scale=1.0 if n == 1 else -1.0,
                                           bias=cst[:, K_ONE:K_ONE + 1] if n == 1 else 0.0)
                if n < 2:
                    ins.then_inc(seen, 1)
            return ins

        def norm_chunk(l, s, m, col):
            nc.scalar.activation(x_hi[:, m, :], xT[:, m, :], ACT.Copy, scale=cur[:, col + m:col + m + 1]).then_inc(xhi_ready, 1)

        def norm_rstd(l, s):
            steps = Steps(act, act_rms, l * 3 + s, 1)
            rms(rstd[:, :], X[0], 1.0 / D, rstd_ready, steps, norm_sum, l * 3 + (s + 1))
            steps.close()

        act.dma_start(cst[:, 0:K_COS], A["consts"][:, 0:K_COS]).then_inc(consts_in, 16)
        tables(LN_EXP)
        for key, r0, cnt in (("norm_mix", R_MIX, 16), ("norm_ffn", R_FFN, 16), ("norm_ple", R_PLE, 16),
                             ("a_subln", R_SUB, 2), ("g_norm", R_GN, 4), ("b_ga", R_BG, 8)):
            act.dma_start(par[r0:r0 + cnt, :], A[key].rearrange("l (c p) -> (l c) p", p=P)).then_inc(par_in, 16)
        act.dma_start(par[R_FIN:R_FIN + 8, :], A["final_norm"].rearrange("(c p) -> c p", p=P)).then_inc(par_in, 16)
        act.dma_start(cst[:, K_COS:NCONST], A["consts"][:, K_COS:NCONST]).then_inc(tables_in, 16)
        for t in range(2):
            act.wait_ge(raw_in[0], 32)
            nc.scalar.copy(w_hi[:, t, :, :], w_raw[:, 0, :, t * P:(t + 1) * P]).then_inc(hi_ready, 1)
        act.wait_ge(consts_in, 16)
        act.wait_ge(lsum_ready, 1)
        nc.scalar.activation(lexp[:, :, :], lsum[:, :, :], ACT.Exp).then_inc(lexp_ready, 1)

        with act.Fori(0, DEPTH) as l:
            tables(LN_EXP)
            act.wait_ge(cur_ready, l + 1)
            act.wait_ge(x_ready, l * 24 + KC)
            for m in range(KC):
                norm_chunk(l, 0, m, U_MIX)
            norm_rstd(l, 0)
            act.wait_ge(zg_ready, l + 1)
            steps = Steps(act, act_decay, l * 2, 2)
            steps.put(nc.scalar.activation(lg, zg[:, :, :], ACT.Abs))
            steps.wait()
            steps.put(nc.scalar.activation(lg, lg, ACT.Exp, scale=-1.0))
            steps.wait()
            steps.close()
            nc.scalar.activation(lg, lg, ACT.Ln, bias=cst[:, K_ONE:K_ONE + 1]).then_inc(lg_ready, 1)

            with act.Fori(0, MIX_IT) as j:
                tb, tb8 = base(l, j, MIX_N, 0)
                v = act.snap(l * MIX_IT + j + 1)
                st = Steps(act, act_mix, v * 5 - 5, 5)

                def at(per, k):
                    return v * per + (k - per)

                def exps(h):
                    act.wait_ge(negmax_ready, at(2, h + 1))
                    if h:
                        act.wait_ge(att_trans, at(2, 1))
                    for n, (dst, src) in enumerate(((p0[:, 0, :], X[4][:, 2 * P:3 * P]), (p0[:, 1, :], X[5][:, 2 * P:3 * P]),
                                                    (p1[:, 0, :], X[4][:, 0:2 * P]), (p1[:, 1, :], X[5][:, 0:2 * P]),
                                                    (p_s[:, :], X[0][:, 0:PAST + TS]))):
                        nc.scalar.activation(dst, src, ACT.Exp, bias=nb[:, n:n + 1], scale=DH ** -0.5,
                                             accum_out=sums[:, n:n + 1]).then_inc(probs_ready, 1)

                def att_copy(h):
                    act.wait_ge(att_trans, at(2, h + 1))
                    if h:
                        act.wait_ge(pv_done, at(2, 1))
                    nc.scalar.copy(attT[:, P:P + 384], X[4][:, 0:384]).then_inc(att_copied, 1)
                    nc.scalar.copy(attT[0:TS, 512:576], X[4][0:TS, 384:448]).then_inc(att_copied, 1)
                    nc.scalar.copy(attT[:, 0:P], X[0][:, 0:P]).then_inc(att_copied, 1)

                def o_copy(h, src):
                    act.wait_ge(pv_done, at(2, h + 1))
                    nc.scalar.copy(o_sb[:, h, :], src[:, 0:T]).then_inc(o_squared, 1)
                    if h:
                        act.wait_ge(o_sum, at(2, 1))
                    nc.scalar.activation(o_sq[:, :], src[:, 0:T], ACT.Square).then_inc(o_squared, 1)

                def tok_copy(dst, src, h, done):
                    nc.scalar.copy(dst[:, 0:2, h * P:(h + 1) * P], src[:, 0:2 * P].rearrange("p (a b) -> p a b", a=2)).then_inc(done, 1)
                    nc.scalar.copy(dst[0:TS, 2, h * P:(h + 1) * P], src[0:TS, 2 * P:3 * P]).then_inc(done, 1)

                for t in range(MIX_N):
                    hi(tb, tb8, t + 2, KC)
                    if t == 3:
                        act.wait_ge(args_ready, v * (2 * NL + 1))
                        nc.scalar.activation(E[:, 0:NL + 1, :], E[:, 0:NL + 1, :], ACT.Exp).then_inc(decay_ready, 1)
                        nc.scalar.activation(E[:, NL + 1, :], E[:, NL + 1, :], ACT.Exp).then_inc(decay_ready, 1)
                    if t == 5:
                        act.wait_ge(stores_left, v)
                        for h in range(2):
                            act.wait_ge(k_trans, at(4, 1 + h))
                            tok_copy(k_tok, X[1 + h], h, k_copied)
                        act.wait_ge(k_trans, at(4, 3))
                        nc.scalar.copy(kcT[:, :, :], X[3][:, :].rearrange("p (a b) -> p a b", a=2)).then_inc(k_copied, 1)
                    if t == 7:
                        exps(0)
                        act.wait_ge(k_trans, at(4, 4))
                        tok_copy(kdT, X[3], 0, k_copied)
                    if t == 10:
                        for e in range(2):
                            act.wait_ge(vg_trans, at(2, e + 1))
                            tok_copy(vg_tok, (X[5], X[1])[e], e, vg_copied)
                        att_copy(0)
                    if t == 11:
                        for h in range(2):
                            act.wait_ge(v_trans, at(2, h + 1))
                            tok_copy(v_tok, X[1 + h], h, v_copied)
                        exps(1)
                    if t == 12:
                        act.wait_ge(result_read, l * RESULTS + j * MIX_N + (12 + CREDIT_RES))
                        st.put(nc.scalar.activation(sig[:, :, :], zr[:, :, :], ACT.Exp, scale=-1.0))
                        st.wait()
                        st.put(nc.scalar.activation(sig[:, :, :], sig[:, :, :], ACT.Ln, bias=cst[:, K_ONE:K_ONE + 1]))
                        st.wait()
                        nc.scalar.activation(sig[:, :, :], sig[:, :, :], ACT.Exp, scale=-1.0).then_inc(sig_ready, 1)
                    if t == 13:
                        o_copy(0, X[1])
                    if t == 14:
                        att_copy(1)
                    if t == 15:
                        for e in range(2):
                            act.wait_ge(og_done, at(2, e + 1))
                            nc.scalar.activation(og_q[:, e, :], X[2 + e][:, 0:T], ACT.Square).then_inc(og_squared, 1)
                        wait_plain(act, consts_in, result_read, l * RESULTS + j * MIX_N + (14 + CREDIT_RES))
                        sigmoid(gab[:, bass.ds(j * 2, 2), :], act_gate, l * (4 * MIX_IT) + j * 2).then_inc(gates_ready, 1)
                        rms(rs[:, 0, :], X[1], 1.0 / DV, o_rstd, st, o_sum, at(2, 1))
                o_copy(1, X[0])
                rms(rs[:, 2, :], X[4], 1.0 / GDV, og_rstd, st, og_sum, v)
                rms(rs[:, 1, :], X[5], 1.0 / DV, o_rstd, st, o_sum, at(2, 2))
                st.close()

            def gate_b(l, j):
                wait_plain(act, consts_in, result_read, l * RESULTS + (RES_MRG + CREDIT_RES))
                sigmoid(gab[:, 2 * j + KC:2 * j + KC + 2, :], act_gate,
                        l * (4 * MIX_IT) + (2 * MIX_IT + 2 * j)).then_inc(gates_ready, 1)

            for n, c in enumerate(list(range(KC, 2 * KC)) + list(range(KC))):
                if n == 0:
                    act.wait_ge(tile_done, l * TILES + (MRG_0 + CREDIT_TILE))
                if n in (0, KC - 2, KC):
                    act.wait_ge(branch_ready, l * (3 * MIX_IT) + 3 * MIX_IT - {0: 3, KC - 2: 1, KC: 0}[n])
                nc.scalar.copy((x_hi[:, c - KC, :] if c >= KC else a_hi[:, c, :]), oag[:, c, :]).then_inc(bhi_ready, 1)
                if n == KC - 1:
                    gate_b(l, 0)
            for j in range(MRG_IT):
                tb, tb8 = base(l, j, MRG_N, MRG_0)
                for t in range(MRG_N):
                    hi(tb, tb8, t + 2, KC)
                    if t == 2 and j < MRG_IT - 1:
                        gate_b(l, j + 1)
                wait_plain(act, consts_in, mixed_ready, l * MRG_IT + j + 1)
                nc.scalar.copy(mix_hi[:, j * 2:j * 2 + 2, :], m2[:, :, :]).then_inc(mixhi_ready, 1)
            for j in range(OUT_IT):
                tb, tb8 = base(l, j, OUT_N, OUT_0)
                for t in range(OUT_N):
                    hi(tb, tb8, t + 2, KC)
                    if m := j * OUT_N + t:
                        act.wait_ge(x_ready, l * 24 + (8 + m))
                        norm_chunk(l, 1, m - 1, U_FFN)

            act.wait_ge(x_ready, l * 24 + (8 + KC))
            norm_chunk(l, 1, KC - 1, U_FFN)
            def up(j, first):
                tb, tb8 = base(l, j, FUP_N, FUP_0)
                for t in range(FUP_N):
                    hi(tb, tb8, t + 2, KC)
                    if first and t == 0:
                        norm_rstd(l, 1)
                        tables(SILU)
                    if t == 2:
                        act.wait_ge(result_read, l * RESULTS + j * FUP_N + (RES_FUP + 2 + CREDIT_RES))
                        nc.scalar.activation(f1z[:, :, :], f1z[:, :, :], ACT.Silu).then_inc(silu_ready, 1)
                wait_plain(act, consts_in, h_ready, l * FUP_IT + j + 1)
                nc.scalar.copy(h_hi[:, bass.ds(j * 2, 2), :], f3z[:, :, :]).then_inc(hhi_ready, 1)

            up(0, True)
            with act.Fori(1, FUP_IT) as j:
                up(j, False)
            for c in range(2):
                act.wait_ge(pe_trans, l * 2 + (c + 1))
                nc.scalar.copy(peT[:, c, :], X[3 + c][:, 0:T]).then_inc(peT_ready, 1)
            for j in range(FDN_IT):
                tb, tb8 = base(l, j, FDN_N, FDN_0)
                for t in range(FDN_N):
                    hi(tb, tb8, t + 2, FDN_K[(t + 2) // 2 % 3])
                    m = j * 4 + t // 6 * 2 + t % 2
                    if t // 2 % 3 == 2 and m:
                        act.wait_ge(x_ready, l * 24 + (16 + m))
                        norm_chunk(l, 2, m - 1, U_PLE)

            tables(LN_EXP)
            act.wait_ge(x_ready, l * 24 + (16 + KC))
            norm_chunk(l, 2, KC - 1, U_PLE)
            for j in range(PLE_IT):
                tb, tb8 = base(l, j, PLE_N, PLE_0)
                for t in range(PLE_N):
                    hi(tb, tb8, t + 2, KC)
                    if j == t == 0:
                        norm_rstd(l, 2)
                        tables(SIGMOID)
                    act.wait_ge(gz_ready, l * KC + j * PLE_N + (t + 1 + CREDIT_RES))
                    nc.scalar.activation(gs[:, :], gz[:, :], ACT.Sigmoid).then_inc(gs_ready, 1)

        tables(LN_EXP)
        steps = Steps(act, act_rms, 3 * DEPTH, 1)
        rms(rstd[:, :], X[0], 1.0 / D, rstd_ready, steps, norm_sum, 3 * DEPTH + 1)
        for t in range(3):
            act.wait_ge(y_trans, t + 1)
            nc.scalar.copy(x_tok[0:rows(t), t, 0:512], X[2 * t][0:rows(t), :]).then_inc(y_copied[1], 1)

    @block.vector
    def _(dve):
        dve.sem_inc(lo_ready, CREDIT_TILE)
        dve.sem_inc(result_read, CREDIT_RES)
        dve.sem_inc(ple_used, 2)
        dve.sem_inc(gz_ready, CREDIT_RES)
        tt = nc.vector.tensor_tensor
        stt = nc.vector.scalar_tensor_tensor

        def lo(tb, t, nk):
            dve.wait_ge(hi_ready, tb + (t + 1))
            tt(w_lo[:, t % 4, 0:nk, :], w_raw[:, (t // 2) % 2, 0:nk, (t % 2) * P:(t % 2 + 1) * P],
               w_hi[:, t % 4, 0:nk, :].bitcast(F32), ALU.subtract).then_inc(lo_ready, 1)

        def lo_chunk(l, s, m, col):
            dve.wait_ge(xhi_ready, l * 24 + (8 * s + m + 1))
            stt(x_lo[:, m, :], xT[:, m, :], cur[:, col + m:col + m + 1], x_hi[:, m, :].bitcast(F32),
                ALU.mult, ALU.subtract).then_inc(xlo_ready, 1)

        st = Steps(dve, dve_pro, 0, 7)
        for m in range(KC):
            dve.wait_ge(x_trans, m + 1)
            nc.vector.tensor_copy(xT[:, m, :], X[m % 4][:, 0:T]).then_inc(x_ready, 1)
        dve.wait_ge(consts_in, 16)
        dve.wait_ge(par_trans, 1)
        st.put(tt(parT[:, :], X[4][:, 0:NPAR], cst[:, K_GS:K_GS + NPAR], ALU.mult))
        dve.wait_ge(lam_in, 64)
        for n in range(2):
            st.put(tt(lprod[:, n, :], lrow[:, 2 * n, :], lrow[:, 2 * n + 1, :], ALU.mult))
        st.wait()
        nc.vector.tensor_reduce(lsum[:, :, :], lprod[:, :, :].rearrange("p a (l d) -> p a l d", l=DEPTH), AX.X, ALU.add).then_inc(lsum_ready, 1)
        dve.wait_ge(lexp_ready, 1)
        st.put(tt(lneg[:, :], lexp[:, 1, :], lexp[:, 0, :], ALU.subtract))
        st.wait()
        tt(lneg[:, :], lneg[:, :], cst[0:1, K_LI:K_LI + DEPTH], ALU.subtract).then_inc(lneg_ready, 1)
        dve.wait_ge(lam_bc, 1)
        st.put(nc.vector.tensor_copy(nlam[:, :], X[5][:, 0:DEPTH]))
        st.wait()
        for l in range(DEPTH):
            st.put(stt(c5[:, l, :], cst[:, K_B5:K_B5 + 5], nlam[:, l:l + 1], cst[:, K_A5:K_A5 + 5], ALU.mult, ALU.add))
        st.close()
        for t in range(2):
            lo(0, t, KC)
        st.wait()
        dve.wait_ge(tables_in, 16)

        with dve.Fori(0, DEPTH) as l:
            dve.wait_ge(ag_in, l * 32 + 32)
            tt(w_agg[:, :, :], w_ag[:, :, :], bc(parT[:, bass.ds(l * KC + R_MIX, KC), None], [P, KC, RANK]), ALU.mult).then_inc(agg_ready, 1)
            for dst, src, n in ((U_MIX, R_MIX, 8), (U_FFN, R_FFN, 8), (U_PLE, R_PLE, 8), (U_SUB, R_SUB, 1),
                                (U_GN, R_GN, 2), (U_BG, R_BG, 4)):
                nc.vector.tensor_copy(cur[:, dst:dst + n], parT[:, bass.ds(l * n + src, n)])
            nc.vector.tensor_copy(cur[:, None, U_C5:U_C5 + 5], c5[:, bass.ds(l, 1), :]).then_inc(cur_ready, 1)
            dve.wait_ge(cur_ready, l + 1)
            for m in range(KC):
                lo_chunk(l, 0, m, U_MIX)
            dve.wait_ge(ag_done, l + 1)
            dve.wait_ge(rstd_ready, l * 3 + 1)
            tt(agT[:, :], X[1][0:RANK, 0:T], rstd[0:RANK, :], ALU.mult).then_inc(agT_ready, 1)
            dve.wait_ge(g_done, l + 1)
            for h in range(GH):
                ins = nc.vector.tensor_scalar(zg[:, h, :], X[2 + h][:, 0:T], cur[:, U_BG + h:U_BG + h + 1], None, ALU.add)
            ins.then_inc(zg_ready, 1)
            with dve.Fori(0, MIX_IT) as j:
                tb = dve.snap(l * TILES + j * MIX_N)
                rb = dve.snap(l * RESULTS + j * MIX_N)
                v = dve.snap(l * MIX_IT + j + 1)
                st = Steps(dve, dve_mix, v * 19 - 19, 19)

                def at(per, k):
                    return v * per + (k - per)

                def result(t):
                    dve.wait_ge(tile_done, tb + (t + 1 + CREDIT_TILE))

                def out_tile(dst, t):
                    result(t)
                    tt(dst, big[t % 2][:, 0:T], rstd[:, :], ALU.mult).then_inc(result_read, 1)

                def written(t):
                    wait_plain(dve, consts_in, result_read, rb + (t + 1 + CREDIT_RES))

                def rope(dst, n):
                    nc.vector.stream_shuffle(rot[:, :, :], z[:, :, :], SWAP).then_inc(shuffled, 1)
                    st.put(tt(dst[:, :, :], z[:, :, :], cos2, ALU.mult))
                    st.wait()
                    dve.wait_ge(sin_ready, at(2, n + 1))
                    tt(dst[:, :, :], dst[:, :, :], rot[:, :, :], ALU.add).then_inc(rope_ready, 1)

                def negmax(h):
                    dve.wait_ge(scores_done, at(2, h + 1))
                    for m in range(2):
                        nc.vector.tensor_reduce(mx[:, m:m + 1], X[4 + m][:, 2 * P:3 * P], AX.X, ALU.max)
                        nc.vector.tensor_reduce(mx[:, 2 + m:3 + m], X[4 + m][:, 0:2 * P], AX.X, ALU.max)
                    st.put(nc.vector.tensor_reduce(mx[:, 4:5], X[0][:, 0:PAST + TS], AX.X, ALU.max))
                    st.wait()
                    nc.vector.tensor_scalar(nb[:, :], mx[:, :], -DH ** -0.5, None, ALU.mult).then_inc(negmax_ready, 1)

                def difference(h):
                    dve.wait_ge(probs_ready, at(10, 5 * h + 5))
                    st.put(nc.vector.reciprocal(coef[:, :], sums[:, :]))
                    st.wait()
                    st.put(tt(coef[:, :], coef[:, :], cur[:, U_C5:U_C5 + 5], ALU.mult))
                    st.wait()
                    nc.vector.tensor_scalar(p0[:, 0, :], p0[:, 0, :], coef[:, 0:1], None, ALU.mult)
                    st.put(nc.vector.tensor_scalar(p1[:, 0, :], p1[:, 0, :], coef[:, 2:3], None, ALU.mult))
                    st.wait()
                    stt(p0[:, 0, :], p0[:, 1, :], coef[:, 1:2], p0[:, 0, :], ALU.mult, ALU.add)
                    stt(p1[:, 0, :], p1[:, 1, :], coef[:, 3:4], p1[:, 0, :], ALU.mult, ALU.add)
                    nc.vector.tensor_scalar(dmat[:, :], cst[:, K_ID2:K_ID2 + TS], coef[:, 4:5], None, ALU.mult).then_inc(maps_ready, 1)

                def state(c, dst, old, src):
                    stt(dst, old, ebl[:, c:c + 1], src, ALU.mult, ALU.add).then_inc(state_ready, 1)
                    dve.wait_ge(state_ready, at(5, {0: 1, 1: 2, 2: 3, 3: 4, 4: 5}[c]))

                for t in range(MIX_N):
                    lo(tb, t + 2, KC)
                    if t == 0:
                        result(0)
                        stt(qg[:, :], big[0][:, 0:T], GDK ** -0.5, rstd[:, :], ALU.mult, ALU.mult).then_inc(result_read, 1)
                    if t == 1:
                        out_tile(kg[:, :], t)
                        wait_plain(dve, consts_in, lg_ready, l + 1)
                        st.put(stt(E[:, NL:NL + 1, :], zg[:, bass.ds(j, 1), :], 0.0, gab[:, bass.ds(j + (2 * KC - GH), 1), :], ALU.min, ALU.subtract))
                        st.wait()
                        st.put(nc.vector.tensor_tensor_scan(E[:, NL + 1, :], cst[:, K_RST:K_RST + T], E[:, NL, :], 0.0, ALU.mult, ALU.add))
                        st.wait()
                        nc.vector.tensor_scalar(E[:, NL + 1, :], E[:, NL + 1, :], 1.0 / 16.0, None, ALU.mult).then_inc(bcur_ready, 1)
                    if t == 2:
                        out_tile(z[:, 0, :], t)
                    if t == 3:
                        out_tile(z[:, 1, :], t)
                        written(3)
                        rope(kr, 0)
                    if t == 4:
                        out_tile(z[:, 0, :], t)
                    if t == 5:
                        out_tile(z[:, 1, :], t)
                        written(5)
                        rope(qr, 1)
                    if t in (6, 7):
                        if t == 7:
                            negmax(0)
                        out_tile(vgT[:, t - 6, :], t)
                    if t == 6:
                        dve.wait_ge(decay_ready, 2 * v)
                        st.put(nc.vector.tensor_copy(ebl[:, :], E[:, NL + 1, CH - 1::CH]))
                        for lev, h in enumerate(LEVELS):
                            (e1, e2), (k1, _), (_, q2) = halves(E[:, lev, :], h), halves(kg[:, :], h), halves(qg[:, :], h)
                            tt(e1, e1, k1, ALU.mult)
                            tt(e2, e2, q2, ALU.mult)
                        tt(E[:, NL, :], E[:, NL, :], kg[:, :], ALU.mult)
                        st.wait()
                        tt(E[:, NL + 1, :], E[:, NL + 1, :], qg[:, :], ALU.mult).then_inc(gla_qk_ready, 1)
                    if t in (8, 9):
                        if t == 8:
                            difference(0)
                            for pair in range(3):
                                if pair == 1:
                                    out_tile(vz[:, 0, :], t)
                                n = rows(pair)
                                dve.wait_ge(pairs_done, at(3, pair + 1))
                                if pair:
                                    dve.wait_ge(a_ready, at(3, pair))
                                st.put(tt(a_msk[0:n, :, :], X[1 + pair][0:n, 0:(NL + 1) * CH].rearrange("p (a b) -> p a b", a=NL + 1),
                                          amask[0:n, :, :], ALU.mult))
                                st.wait()
                                nc.vector.tensor_reduce(a_sum[0:n, pair, :], a_msk[0:n, :, :].rearrange("p a b -> p b a"), AX.X, ALU.add).then_inc(a_ready, 1)
                        if t == 9:
                            out_tile(vz[:, 1, :], t)
                    if t in (10, 11):
                        if t == 10:
                            dve.wait_ge(vg_trans, 2 * v)
                        else:
                            negmax(1)
                        out_tile(zr[:, t - 10, :], t)
                    if t >= 12:
                        if t == 12:
                            dve.wait_ge(stores_left, v)
                            dve.wait_ge(u_done, at(3, 1))
                            nc.vector.tensor_copy(S[:, 0, :], X[3][:, 0:GDV]).then_inc(state_ready, 1)
                            dve.wait_ge(state_ready, at(5, 1))
                            difference(1)
                        if t == 13:
                            dve.wait_ge(u_done, at(3, 2))
                            state(1, S[:, 1, :], S[:, 0, :], X[2][:, 0:GDV])
                            state(2, S[:, 2, :], S[:, 1, :], X[3][:, GDV:2 * GDV])
                            state(3, S[:, 3, :], S[:, 2, :], X[2][:, GDV:2 * GDV])
                        if t == 14:
                            dve.wait_ge(u_done, at(3, 3))
                            dve.wait_ge(s_past_in, 16 * v)
                            state(4, S_smp[:, :], s_past[:, :], X[5][:, 0:GDV])
                        if t == 15:
                            dve.wait_ge(sig_ready, v)
                            st.put(tt(zr[:, :, :], zr[:, :, :], sig[:, :, :], ALU.mult))
                        c = (t - 12) if t < 14 else (KC + t - 14)
                        result(t)
                        tt(gab[:, bass.ds(j * 2 + c, 1), :], big[t % 2][:, None, 0:T], rstd[:, None, :], ALU.mult).then_inc(result_read, 1)
                def head_out(h):
                    dve.wait_ge(o_rstd, at(2, h + 1))
                    stt(oag[:, bass.ds(j * 2 + h, 1), :], o_sb[:, h:h + 1, :], cur[:, U_SUB:U_SUB + 1], rs[:, h:h + 1, :],
                        ALU.mult, ALU.mult).then_inc(branch_ready, 1)
                head_out(0)
                dve.wait_ge(og_rstd, v)
                for e in range(2):
                    st.put(stt(og_t[:, e, :], X[2 + e][:, 0:T], cur[:, U_GN + e:U_GN + e + 1], rs[:, 2, :], ALU.mult, ALU.mult))
                st.wait()
                tt(oag[:, bass.ds(j * 2 + KC, 2), :], og_t[:, :, :], zr[:, :, :], ALU.mult).then_inc(branch_ready, 1)
                head_out(1)
                st.close()

            for n, c in enumerate(list(range(KC, 2 * KC)) + list(range(KC))):
                dve.wait_ge(bhi_ready, l * (2 * KC) + (n + 1))
                to, hi = (x_lo[:, c - KC, :], x_hi[:, c - KC, :]) if c >= KC else (a_lo[:, c, :], a_hi[:, c, :])
                tt(to, oag[:, c, :], hi.bitcast(F32), ALU.subtract).then_inc(blo_ready, 1)
            with dve.Fori(0, MRG_IT) as j:
                tb = dve.snap(l * TILES + j * MRG_N + MRG_0)
                rb = dve.snap(l * RESULTS + j * MRG_N + RES_MRG)
                for t in range(MRG_N):
                    lo(tb, t + 2, KC)
                    if t == 0:
                        wait_plain(dve, consts_in, gates_ready, l * (2 * MIX_IT) + j + (MIX_IT + 1))
                    dve.wait_ge(tile_done, tb + (t + 1 + CREDIT_TILE))
                    c = t % 2 + (KC if t < 2 else 0)
                    tt((m1 if t < 2 else m2)[:, t % 2:t % 2 + 1, :], big[t % 2][:, None, 0:T], gab[:, bass.ds(j * 2 + c, 1), :],
                       ALU.mult).then_inc(result_read, 1)
                dve.wait_ge(result_read, rb + (MRG_N + CREDIT_RES))
                tt(m2[:, :, :], m2[:, :, :], m1[:, :, :], ALU.add).then_inc(mixed_ready, 1)
                dve.wait_ge(mixed_ready, l * MRG_IT + j + 1)
                dve.wait_ge(mixhi_ready, l * MRG_IT + j + 1)
                tt(mix_lo[:, bass.ds(j * 2, 2), :], m2[:, :, :], mix_hi[:, bass.ds(j * 2, 2), :].bitcast(F32), ALU.subtract).then_inc(mixlo_ready, 1)
            for j in range(OUT_IT):
                tb = dve.snap(l * TILES + j * OUT_N + OUT_0)
                for t in range(OUT_N):
                    lo(tb, t + 2, KC)
                    dve.wait_ge(tile_done, tb + (t + 1 + CREDIT_TILE))
                    m = j * 4 + t
                    x = xT[:, m, :]
                    tt(x, big[t % 2][:, 0:T], x, ALU.add).then_inc(x_ready, 1)
                    if m:
                        lo_chunk(l, 1, m - 1, U_FFN)

            lo_chunk(l, 1, KC - 1, U_FFN)
            def up(j, first):
                tb = dve.snap(l * TILES + j * FUP_N + FUP_0)
                rb = dve.snap(l * RESULTS + j * FUP_N + RES_FUP)
                for t in range(FUP_N):
                    lo(tb, t + 2, KC)
                    if first and t == 0:
                        dve.wait_ge(rstd_ready, l * 3 + 2)
                    dve.wait_ge(tile_done, tb + (t + 1 + CREDIT_TILE))
                    tt((f1z if t < 2 else f3z)[:, t % 2, :], big[t % 2][:, 0:T], rstd[:, :], ALU.mult).then_inc(result_read, 1)
                dve.wait_ge(result_read, rb + (FUP_N + CREDIT_RES))
                dve.wait_ge(silu_ready, l * FUP_IT + j + 1)
                tt(f3z[:, :, :], f3z[:, :, :], f1z[:, :, :], ALU.mult).then_inc(h_ready, 1)
                dve.wait_ge(h_ready, l * FUP_IT + j + 1)
                dve.wait_ge(hhi_ready, l * FUP_IT + j + 1)
                tt(h_lo[:, bass.ds(j * 2, 2), :], f3z[:, :, :], h_hi[:, bass.ds(j * 2, 2), :].bitcast(F32), ALU.subtract).then_inc(hlo_ready, 1)

            up(0, True)
            with dve.Fori(1, FUP_IT) as j:
                up(j, False)
            for j in range(FDN_IT):
                tb = dve.snap(l * TILES + j * FDN_N + FDN_0)
                for t in range(FDN_N):
                    lo(tb, t + 2, FDN_K[(t + 2) // 2 % 3])
                    if t // 2 % 3 == 2:
                        dve.wait_ge(tile_done, tb + (t + 1 + CREDIT_TILE))
                        m = j * 4 + t // 6 * 2 + t % 2
                        x = xT[:, m, :]
                        tt(x, big[t % 2][:, 0:T], x, ALU.add).then_inc(x_ready, 1)
                        if m:
                            lo_chunk(l, 2, m - 1, U_PLE)

            lo_chunk(l, 2, KC - 1, U_PLE)
            for j in range(PLE_IT):
                tb = dve.snap(l * TILES + j * PLE_N + PLE_0)
                n8 = dve.snap(l * KC + j * PLE_N)
                for t in range(PLE_N):
                    lo(tb, t + 2, KC)
                    if j == t == 0:
                        dve.wait_ge(rstd_ready, l * 3 + 3)
                    dve.wait_ge(tile_done, tb + (t + 1 + CREDIT_TILE))
                    tt(gz[:, :], big[t % 2][:, 0:T], rstd[:, :], ALU.mult).then_inc(gz_ready, 1)
                    dve.wait_ge(gs_ready, n8 + (t + 1))
                    dve.wait_ge(ple_done, n8 + (t + 1))
                    tt(gs[:, :], gs[:, :], X[1 + t % 2][:, 0:T], ALU.mult).then_inc(ple_used, 1)
                    dve.wait_ge(ple_used, n8 + (t + 1 + 2))
                    x = xT[:, j * 4 + t, :]
                    tt(x, x, gs[:, :], ALU.add).then_inc(x_ready, 1)

        dve.wait_ge(rstd_ready, 3 * DEPTH + 1)
        for m in range(KC):
            stt(xT[:, m, :], xT[:, m, :], parT[:, R_FIN + m:R_FIN + m + 1], rstd[:, :], ALU.mult, ALU.mult).then_inc(y_ready, 1)
        for t in range(3):
            dve.wait_ge(y_trans, 3 + t + 1)
            nc.vector.tensor_copy(x_tok[0:rows(t), t, 512:1024], X[2 * t + 1][0:rows(t), :]).then_inc(y_copied[0], 1)

    @block.tensor
    def _(pe):
        mm = nc.tensor.matmul
        pe.sem_inc(tile_done, CREDIT_TILE)

        def tile(tb, t, xh, xl, k0=0, nk=KC, start=True, stop=True, chunk_wait=None, per=1, between=()):
            pe.wait_ge(lo_ready, tb + (t + 1 + CREDIT_TILE))
            out = big[t % 2][:, 0:T]
            between = iter(between)
            for k in range(nk):
                if chunk_wait is not None:
                    pe.wait_ge(chunk_wait[0], chunk_wait[1] + (k // per + 1))
                wh, wl = w_hi[:, t % 4, k, :], w_lo[:, t % 4, k, :]
                mm(out, wh, xh[:, k0 + k, :], start=start and k == 0, stop=False)
                mm(out, wh, xl[:, k0 + k, :], start=False, stop=False)
                last = mm(out, wl, xh[:, k0 + k, :], start=False, stop=stop and k == nk - 1)
                if k == nk - 1:
                    last.then_inc(tile_done, 1)
                next(between, None)

        def transposes(out, srcs):
            for i in range(3):
                last = nc.tensor.transpose(out[0:rows(i), i * P:(i + 1) * P], srcs[:, i * P:i * P + rows(i)], ident)
            return last

        def norm_sums(count):
            pe.wait_ge(ssq_ready, count)
            mm(X[0][:, 0:T], ones, ssq[:, :], start=True, stop=True).then_inc(norm_sum, 1)

        pe.wait_ge(consts_in, 16)
        for m in range(KC):
            if m % 4 == 0:
                pe.wait_ge(x_in[m // 4], 32)
            if m >= 4:
                pe.wait_ge(x_ready, m - 3)
            for i in range(3):
                n = rows(i)
                last = nc.tensor.transpose(X[m % 4][:, i * P:i * P + n], x_tok[0:n, i, m * P:(m + 1) * P], ident[0:n, 0:n])
            last.then_inc(x_trans, 1)
        pe.wait_ge(par_in, 112)
        nc.tensor.transpose(X[4][:, 0:NPAR], par[:, :], ident[0:NPAR, 0:NPAR]).then_inc(par_trans, 1)
        pe.wait_ge(lneg_ready, 1)
        mm(X[5][:, 0:DEPTH], ones[0:1, :], lneg[:, :], start=True, stop=True).then_inc(lam_bc, 1)

        pe.wait_ge(tables_in, 16)
        with pe.Fori(0, DEPTH) as l:
            pe.wait_ge(x_ready, l * 24 + 8)
            pe.wait_ge(agg_ready, l + 1)
            for k in range(KC):
                last = mm(X[1][0:RANK, 0:T], w_agg[:, k, :], xT[:, k, :], start=k == 0, stop=k == KC - 1)
            last.then_inc(ag_done, 1)
            norm_sums(l * 3 + 1)
            pe.wait_ge(agT_ready, l + 1)
            for h in range(GH):
                last = mm(X[2 + h][:, 0:T], ga2[:, h * GDK:(h + 1) * GDK], agT[:, :], start=True, stop=True)
            last.then_inc(g_done, 1)

            with pe.Fori(0, MIX_IT) as j:
                tb = pe.snap(l * TILES + j * MIX_N)
                rb = pe.snap(l * RESULTS + j * MIX_N)
                v = pe.snap(l * MIX_IT + j + 1)
                xc = pe.snap(l * 24)

                def at(per, k):
                    return v * per + (k - per)

                def scores(h):
                    q, k, kc = qr[:, h, :], kr[:, h, :], kcT[:, h, :]
                    mq = cst[0:1, K_MQ:K_MQ + P]
                    yield
                    yield
                    if h == 0:
                        pe.wait_ge(rope_ready, 2 * v)
                        pe.wait_ge(k_copied, at(7, 5))
                    else:
                        pe.wait_ge(att_copied, at(6, 3))
                    for at0, q0, nk in ((0, P, 2 * P), (2 * P, 0, P)):
                        for m in range(2):
                            r = slice(m * DH, (m + 1) * DH)
                            mm(X[4 + m][:, at0:at0 + nk - CH], q[r, q0:q0 + P], k[r, 0:nk - CH], start=True, stop=True)
                        yield
                        for m in range(2):
                            r = slice(m * DH, (m + 1) * DH)
                            mm(X[4 + m][:, at0 + nk - CH:at0 + nk], q[r, q0:q0 + P], k[r, nk - CH:nk], start=True, stop=False)
                        for m in range(2):
                            mm(X[4 + m][:, at0 + nk - CH:at0 + nk], mq, cst[0:1, K_ONE:K_ONE + CH], start=False, stop=True)
                        yield
                    for at0, keys in ((0, kc), (PAST, k[:, TP:T])):
                        if at0:
                            yield
                        for m in range(2):
                            r = slice(m * DH, (m + 1) * DH)
                            last = mm(X[0][r, at0:at0 + (PAST if at0 == 0 else TS)], q[r, TP:T], keys[r, :], start=True, stop=True)
                    last.then_inc(scores_done, 1)

                def att_transposes(h):
                    out = X[4]
                    pe.wait_ge(maps_ready, at(2, h + 1))
                    for i in range(2):
                        nc.tensor.transpose(out[:, i * P:(i + 1) * P], p1[:, 0, i * P:(i + 1) * P], ident)
                    nc.tensor.transpose(X[0][:, 0:P], p0[:, 0, :], ident)
                    for i in range(3):
                        n = rows(i)
                        last = mm(out[0:n, 2 * P + i * TS:2 * P + (i + 1) * TS], p_s[:, i * P:i * P + n], dmat[:, :], start=True, stop=True)
                    last.then_inc(att_trans, 1)

                def values(h, out):
                    c = slice(h * P, (h + 1) * P)
                    pe.wait_ge(att_copied, at(6, 3 * h + 3))
                    mm(out[:, 0:P], v_tok[:, 0, c], attT[:, 0:P], start=True, stop=True)
                    mm(out[:, P:2 * P], v_tok[:, 0, c], attT[:, P:2 * P], start=True, stop=False)
                    mm(out[:, P:2 * P], v_tok[:, 1, c], attT[:, 2 * P:3 * P], start=False, stop=True)
                    mm(out[:, TP:T], v_past[:, 0, c], attT[:, 384:448], start=True, stop=False)
                    mm(out[:, TP:T], v_past[:, 1, c], attT[:, 448:512], start=False, stop=False)
                    mm(out[:, TP:T], v_tok[0:TS, 2, c], attT[0:TS, 512:576], start=False, stop=True).then_inc(pv_done, 1)

                def chunk_rows(c):
                    return slice((c % 2) * CH, (c % 2) * CH + CH)

                def own_sum(c, out):
                    return mm(out, kdT[chunk_rows(c), c // 2, :], vg_tok[chunk_rows(c), c // 2, :], start=True, stop=True)

                def gla_outputs():
                    pe.wait_ge(state_ready, at(5, 4))
                    for parity, e in ((0, 0), (0, 1), (1, 0), (1, 1)):
                        if parity:
                            pe.wait_ge(og_even, at(2, e + 1))
                        for c in range(parity, NCH, 2):
                            out = X[2 + e][:, c * CH:(c + 1) * CH]
                            ec = slice(e * P, (e + 1) * P)
                            old = None if c == 0 else (S[:, c - 1, ec] if c < NCH - 1 else s_past[:, ec])
                            if old is not None:
                                if c == NCH - 1:
                                    pe.wait_ge(s_past_in, 16 * v)
                                mm(out, old, E[:, NL + 1, c * CH:(c + 1) * CH], start=True, stop=False)
                            last = mm(out, vg_tok[chunk_rows(c), c // 2, ec], a_sum[chunk_rows(c), c // 2, :],
                                      start=old is None, stop=True)
                        last.then_inc(og_done if parity else og_even, 1)
                        yield
                    pe.wait_ge(o_squared, at(4, 2))
                    mm(X[1][:, 0:T], ones, o_sq[:, :], start=True, stop=True).then_inc(o_sum, 1)

                for t in range(MIX_N):
                    pe.wait_ge(result_read, rb + (t - 1 + CREDIT_RES))
                    tile(tb, t, x_hi, x_lo, chunk_wait=(xlo_ready, xc) if t == 0 else None,
                         between={7: scores(0), 11: scores(1), 15: gla_outputs()}.get(t, ()))
                    if t == 5:
                        pe.wait_ge(rope_ready, at(2, 1))
                        for h in range(2):
                            transposes(X[1 + h], kr[:, h, :]).then_inc(k_trans, 1)
                        pe.wait_ge(k_raw_in, 16 * v)
                        for h in range(2):
                            for i in range(2):
                                last = nc.tensor.transpose(X[3][:, (2 * h + i) * P:(2 * h + i + 1) * P],
                                                           k_raw[:, i, h * P:(h + 1) * P], ident)
                        last.then_inc(k_trans, 1)
                    if t == 7:
                        pe.wait_ge(gla_qk_ready, v)
                        transposes(X[3], E[:, NL, :]).then_inc(k_trans, 1)
                    if t in (7, 8):
                        if t == 8:
                            pe.wait_ge(k_copied, 7 * v)
                        for pair in ((0, 1) if t == 7 else (2,)):
                            for c in range(2 * pair, min(2 * pair + 2, NCH)):
                                cols = slice(c * CH, (c + 1) * CH)
                                for lev in range(NL + 1):
                                    lhs = E[:, lev, cols] if lev < NL else kg[:, cols]
                                    rhs = E[:, lev, cols] if lev < NL else qg[:, cols]
                                    last = mm(X[1 + pair][chunk_rows(c), lev * CH:(lev + 1) * CH], lhs, rhs, start=True, stop=True)
                            last.then_inc(pairs_done, 1)
                    if t == 9:
                        pe.wait_ge(a_ready, at(3, 1))
                        for e, bank in enumerate((X[5], X[1])):
                            transposes(bank, vgT[:, e, :]).then_inc(vg_trans, 1)
                        att_transposes(0)
                    if t == 10:
                        pe.wait_ge(vg_copied, 4 * v)
                        pe.wait_ge(a_ready, at(3, 2))
                        pe.wait_ge(result_read, rb + (10 + CREDIT_RES))
                        for h in range(2):
                            transposes(X[1 + h], vz[:, h, :]).then_inc(v_trans, 1)
                    if t == 11:
                        pe.wait_ge(a_ready, 3 * v)
                        own_sum(0, X[3][:, 0:GDV])
                        own_sum(2, X[3][:, GDV:2 * GDV]).then_inc(u_done, 1)
                    if t == 12:
                        pe.wait_ge(v_copied, 4 * v)
                        pe.wait_ge(v_past_in, 16 * v)
                        values(0, X[1])
                        own_sum(1, X[2][:, 0:GDV])
                        own_sum(3, X[2][:, GDV:2 * GDV]).then_inc(u_done, 1)
                    if t == 13:
                        att_transposes(1)
                        own_sum(4, X[5][:, 0:GDV]).then_inc(u_done, 1)
                    if t == 15:
                        values(1, X[0])
                        pe.wait_ge(og_squared, 2 * v)
                        for e in range(2):
                            last = mm(X[4][:, 0:T], ones, og_q[:, e, :], start=e == 0, stop=e == 1)
                        last.then_inc(og_sum, 1)
                        pe.wait_ge(state_ready, 5 * v)
                        pe.wait_ge(o_squared, 4 * v)
                        mm(X[5][:, 0:T], ones, o_sq[:, :], start=True, stop=True).then_inc(o_sum, 1)

            with pe.Fori(0, MRG_IT) as j:
                tb = pe.snap(l * TILES + j * MRG_N + MRG_0)
                rb = pe.snap(l * RESULTS + j * MRG_N + RES_MRG)
                bc0 = pe.snap(l * (2 * KC))
                for t in range(MRG_N):
                    if t == 2:
                        pe.wait_ge(blo_ready, l * (2 * KC) + 2 * KC)
                    pe.wait_ge(result_read, rb + (t - 1 + CREDIT_RES))
                    xh, xl = (x_hi, x_lo) if t < 2 else (a_hi, a_lo)
                    tile(tb, t, xh, xl, chunk_wait=(blo_ready, bc0) if t == 0 else None)
            for j in range(OUT_IT):
                tb = pe.snap(l * TILES + j * OUT_N + OUT_0)
                for t in range(OUT_N):
                    if j == 0 and t < 2:
                        pe.wait_ge(result_read, l * RESULTS + (RES_FUP - 1 + t + CREDIT_RES))
                    else:
                        pe.wait_ge(x_ready, l * 24 + (j * 4 + 8 + t - 1))
                    tile(tb, t, mix_hi, mix_lo, chunk_wait=(mixlo_ready, l * MRG_IT) if j == t == 0 else None, per=2)

            def up(j, first):
                tb = pe.snap(l * TILES + j * FUP_N + FUP_0)
                rb = pe.snap(l * RESULTS + j * FUP_N + RES_FUP)
                xc = pe.snap(l * 24 + 8)
                for t in range(FUP_N):
                    if first and t < 2:
                        pe.wait_ge(x_ready, l * 24 + (8 + KC - 1 + t))
                    else:
                        pe.wait_ge(result_read, rb + (t - 1 + CREDIT_RES))
                    tile(tb, t, x_hi, x_lo, chunk_wait=(xlo_ready, xc) if first and t == 0 else None)
                    if first and t == 0:
                        norm_sums(l * 3 + 2)

            up(0, True)
            with pe.Fori(1, FUP_IT) as j:
                up(j, False)
            pe.wait_ge(pe_in, l * 32 + 32)
            for c in range(2):
                for i in range(3):
                    n = rows(i)
                    last = nc.tensor.transpose(X[3 + c][:, i * P:i * P + n], pe_tok[0:n, i, c * P:(c + 1) * P], ident[0:n, 0:n])
                last.then_inc(pe_trans, 1)
            with pe.Fori(0, FDN_IT) as j:
                tb = pe.snap(l * TILES + j * FDN_N + FDN_0)
                for t in range(FDN_N):
                    pair, k, mt = t // 6, t // 2 % 3, t % 2
                    if k == 0:
                        pe.wait_ge(result_read, l * RESULTS + (RESULTS - 1 + mt + CREDIT_RES))
                        pe.wait_ge(x_ready, l * 24 + j * 4 + (16 + 2 * pair + mt - 1))
                    if mt == 0:
                        pe.wait_ge(hlo_ready, l * FUP_IT + (4, 8, 11)[k])
                    tile(tb, t, h_hi, h_lo, k0=KC * k, nk=FDN_K[k], start=k == 0, stop=k == 2)

            pe.wait_ge(peT_ready, l * 2 + 2)

            def gate(j, first):
                tb = pe.snap(l * TILES + j * PLE_N + PLE_0)
                n8 = pe.snap(l * KC + j * PLE_N)
                xc = pe.snap(l * 24 + 16)
                for t in range(PLE_N):
                    if t % 2 == 0:
                        pe.wait_ge(wple_in[t // 2], l * (16 * PLE_IT) + j * 16 + 16)
                    pe.wait_ge(ple_used, n8 + (t + 1))
                    for c in range(2):
                        last = mm(X[1 + t % 2][:, 0:T], wple[:, t // 2, c, t % 2 * P:(t % 2 + 1) * P], peT[:, c, :],
                                  start=c == 0, stop=c == 1)
                    last.then_inc(ple_done, 1)
                    if first and t < 2:
                        pe.wait_ge(x_ready, l * 24 + (16 + KC - 1 + t))
                    else:
                        pe.wait_ge(gz_ready, n8 + (t + 1))
                    tile(tb, t, x_hi, x_lo, chunk_wait=(xlo_ready, xc) if first and t == 0 else None)
                    if first and t == 0:
                        norm_sums(l * 3 + 3)

            for j in range(PLE_IT):
                gate(j, j == 0)

        norm_sums(3 * DEPTH + 1)
        for c in range(KC):
            pe.wait_ge(y_ready, c + 1)
            half, m = c // 4, c % 4
            for t in range(3):
                last = nc.tensor.transpose(X[2 * t + half][0:rows(t), m * P:(m + 1) * P], xT[:, c, t * P:t * P + rows(t)], ident)
                if m == 3:
                    last.then_inc(y_trans, 1)

    ctx.close()


OUTS = [("y_prompt", (1, TP, D)), ("y_sample", (1, TS, D)),
        ("k_prompt", (DEPTH, 1, TP, HEADS, DV)), ("v_prompt", (DEPTH, 1, TP, HEADS, DV)),
        ("s_prompt", (DEPTH, 1, GH, GDK, GDV)),
        ("k_sample", (DEPTH, 1, TS, HEADS, DV)), ("v_sample", (DEPTH, 1, TS, HEADS, DV)),
        ("s_sample", (DEPTH, 1, GH, GDK, GDV))]


def constants():
    import math

    import numpy as np
    f = np.float32
    c = np.zeros((P, NCONST), f)
    c[:, K_ID:K_ID + P] = np.eye(P)
    c[:, K_ONE:K_ONE + P] = 1.0
    half = DH // 8
    inv = f(500000.0) ** (-np.arange(0, 2 * half, 2, dtype=f) / f(2 * half))
    ang = np.arange(T, dtype=f)[None, :] * inv[:, None]
    c[:, K_COS:K_COS + T] = 1.0
    for m in range(2):
        for i in range(half):
            a, b = m * DH + i, m * DH + half + i
            c[a, K_COS:K_COS + T] = c[b, K_COS:K_COS + T] = np.cos(ang[i])
            c[a, K_SIN:K_SIN + T] = -np.sin(ang[i])
            c[b, K_SIN:K_SIN + T] = np.sin(ang[i])
    c[:, K_RST:K_RST + T] = np.arange(T) % CH != 0
    k, q = np.arange(CH)[:, None], np.arange(CH)[None, :]
    for lev, h in enumerate(LEVELS + [0]):
        ok = (k == q) if h == 0 else (k // (2 * h) == q // (2 * h)) & (k % (2 * h) < h) & (q % (2 * h) >= h)
        c[:, K_MASK + lev * CH:K_MASK + (lev + 1) * CH] = np.concatenate([ok, ok])
    c[:, K_ID2:K_ID2 + TS] = np.concatenate([np.eye(TS)] * 2)
    c[0, K_MQ:K_MQ + CH] = -1e30
    c[:, K_EPS] = EPS
    c[:, K_GS:K_GS + NPAR] = 1.0
    low = np.arange(P) < DH
    c[:, K_A5:K_A5 + 5] = np.array([1, 0, 1, 0, 0], f)
    c[:, K_B5:K_B5 + 5] = np.array([0, 1, 0, 1, 0], f)
    c[:, K_A5 + 4], c[:, K_B5 + 4] = low, ~low
    for l in range(DEPTH):
        li = 0.8 - 0.6 * math.exp(-0.3 * l)
        c[:, K_LI + l], c[:, K_GS + R_SUB + l] = li, 1.0 - li
    return c


def kernel(**inputs):
    import numpy as np
    import concourse.bacc as bacc
    from concourse.bass_utils import run_bass_kernel_spmd

    nc = bacc.Bacc("TRN2", target_bir_lowering=False, num_devices=1)
    arrays, A, O = {}, {}, {}
    for name, a in list(inputs.items()) + [("consts", constants())]:
        a = np.ascontiguousarray(a)
        arrays[f"in_{name}"] = a
        A[name] = nc.dram_tensor(f"in_{name}", a.shape, F32, kind="ExternalInput").ap()
    for name, shape in OUTS:
        O[name] = nc.dram_tensor(f"out_{name}", shape, F32, kind="ExternalOutput").ap()
    encoder(nc, A, O)
    r = run_bass_kernel_spmd(nc, [arrays], core_ids=[0])
    return tuple(r.results[0][f"out_{name}"] for name, _ in OUTS)
```
